# Optimizing a Trainium2 kernel written in Bass

```python
import math
import jax, jax.numpy as jnp
from jax import lax
import numpy as np

D_MODEL = 2048
BATCH = 1
SEQ = 256
DEPTH = 1

PLE_DIM = 256
D_MIX = D_MODEL
MLSTM_HEADS = 4
MLSTM_HEAD_DIM = (D_MIX // 2) // MLSTM_HEADS
MLSTM_WIDTH = MLSTM_HEADS * MLSTM_HEAD_DIM
MLSTM_CHUNK = 64
FOX_HEADS = 8
FOX_HEAD_DIM = (D_MIX - MLSTM_WIDTH) // FOX_HEADS
FOX_WIDTH = FOX_HEADS * FOX_HEAD_DIM
FOX_BLOCK = 128
D_FF = ((8 * D_MODEL // 3 + 255) // 256) * 256
CONV_WIDTH = 3
EPS = 1e-6
IN_SIZES = (MLSTM_WIDTH, MLSTM_WIDTH, MLSTM_WIDTH, MLSTM_WIDTH, MLSTM_HEADS, MLSTM_HEADS,
            FOX_WIDTH, FOX_WIDTH, FOX_WIDTH, FOX_HEADS)
IN_TOTAL = sum(IN_SIZES)


def rms_norm(x, g):
    xf = x.astype(jnp.float32)
    y = xf * lax.rsqrt(jnp.mean(xf * xf, axis=-1, keepdims=True) + EPS)
    return (y * g.astype(jnp.float32)).astype(x.dtype)

def mlstm_chunkwise(q, k, v, ig, lf):
    B, H, S, d = q.shape
    L = MLSTM_CHUNK
    nc = S // L
    k = k * (d ** -0.5)

    def to_chunks(t):
        return jnp.moveaxis(t.reshape((B, H, nc, L) + t.shape[3:]), 2, 0)

    qc, kc, vc = to_chunks(q), to_chunks(k), to_chunks(v)
    igc = to_chunks(ig)
    bc = jnp.cumsum(to_chunks(lf), axis=-1)
    causal = jnp.tril(jnp.ones((L, L), dtype=bool))

    def step(carry, inp):
        C, n, m = carry
        qi, ki, vi, ii, bi = inp
        inter = bi + m[..., None]
        D = jnp.where(causal, bi[..., :, None] - bi[..., None, :] + ii[..., None, :], -jnp.inf)
        m_comb = jnp.maximum(inter, jnp.max(D, axis=-1))
        w_intra = jnp.exp(D - m_comb[..., None])
        w_inter = jnp.exp(inter - m_comb)
        s = jnp.einsum('bhtd,bhsd->bhts', qi, ki) * w_intra
        num = jnp.einsum('bhts,bhsv->bhtv', s, vi) + w_inter[..., None] * jnp.einsum('bhtk,bhkv->bhtv', qi, C)
        den = jnp.sum(s, axis=-1) + w_inter * jnp.einsum('bhtk,bhk->bht', qi, n)
        h = num / jnp.maximum(jnp.abs(den), jnp.exp(-m_comb))[..., None]
        bL = bi[..., -1]
        g = bL[..., None] - bi + ii
        m_new = jnp.maximum(bL + m, jnp.max(g, axis=-1))
        wk = jnp.exp(g - m_new[..., None])
        decay = jnp.exp(bL + m - m_new)
        C = decay[..., None, None] * C + jnp.einsum('bhsk,bhsv->bhkv', ki * wk[..., None], vi)
        n = decay[..., None] * n + jnp.einsum('bhs,bhsk->bhk', wk, ki)
        return (C, n, m_new), h

    init = (jnp.zeros((B, H, d, d), jnp.float32), jnp.zeros((B, H, d), jnp.float32),
            jnp.zeros((B, H), jnp.float32))
    _, hs = lax.scan(step, init, (qc, kc, vc, igc, bc))
    return jnp.moveaxis(hs, 0, 2).reshape(B, H, S, d)

def forgetting_attention(q, k, v, logf):
    B, S, H, d = q.shape
    nb = S // FOX_BLOCK
    F = jnp.cumsum(logf, axis=1).transpose(0, 2, 1)
    kt = k.transpose(0, 2, 1, 3)
    vt = v.transpose(0, 2, 1, 3)
    qb = q.reshape(B, nb, FOX_BLOCK, H, d).transpose(1, 0, 3, 2, 4)
    Fq = F.reshape(B, H, nb, FOX_BLOCK).transpose(2, 0, 1, 3)
    kpos = jnp.arange(S)
    scale = d ** -0.5

    def one_block(args):
        qi, Fqi, bi = args
        qpos = bi * FOX_BLOCK + jnp.arange(FOX_BLOCK)
        s = jnp.einsum('bhqd,bhkd->bhqk', qi, kt, preferred_element_type=jnp.float32) * scale
        s = s + Fqi[..., None] - F[:, :, None, :]
        s = jnp.where(kpos[None, :] <= qpos[:, None], s, -jnp.inf)
        pr = jax.nn.softmax(s, axis=-1)
        return jnp.einsum('bhqk,bhkd->bhqd', pr.astype(vt.dtype), vt)

    out = lax.map(one_block, (qb, Fq, jnp.arange(nb)))
    return out.transpose(1, 0, 3, 2, 4).reshape(B, S, H * d)

def causal_dwconv(a, w, b):
    y = lax.conv_general_dilated(a, w[:, None, :].astype(a.dtype), window_strides=(1,),
                                 padding=[(CONV_WIDTH - 1, 0)],
                                 dimension_numbers=('NWC', 'WIO', 'NWC'),
                                 feature_group_count=a.shape[-1])
    return y + b.astype(a.dtype)

def first_inputs(seed: int = 0) -> dict:
    key = jax.random.key(seed)
    ks = jax.random.split(key, 20)
    nrm = jax.random.normal
    f32 = jnp.float32
    x = nrm(ks[0], (BATCH, SEQ, D_MODEL), f32)
    p = nrm(ks[1], (DEPTH, BATCH, SEQ, PLE_DIM), f32)
    mix_norm_g = 1.0 + 0.02 * nrm(ks[2], (DEPTH, D_MODEL), f32)
    w_in = nrm(ks[3], (DEPTH, D_MODEL, IN_TOTAL), f32) * D_MODEL ** -0.5
    m_i_bias = 0.1 * nrm(ks[4], (DEPTH, MLSTM_HEADS), f32)
    m_f_bias = jnp.linspace(3.0, 6.0, MLSTM_HEADS, dtype=f32)[None, :] + 0.01 * nrm(ks[5], (DEPTH, MLSTM_HEADS), f32)
    mlstm_gate_bias = jnp.concatenate([m_i_bias, m_f_bias], axis=-1)
    mlstm_out_g = 1.0 + 0.02 * nrm(ks[6], (DEPTH, MLSTM_WIDTH), f32)
    fox_q_g = 1.0 + 0.02 * nrm(ks[7], (DEPTH, FOX_HEAD_DIM), f32)
    fox_k_g = 1.0 + 0.02 * nrm(ks[8], (DEPTH, FOX_HEAD_DIM), f32)
    fox_f_bias = jnp.linspace(1.0, 5.0, FOX_HEADS, dtype=f32)[None, :] + 0.01 * nrm(ks[9], (DEPTH, FOX_HEADS), f32)
    w_out = nrm(ks[10], (DEPTH, D_MIX, D_MODEL), f32) * D_MIX ** -0.5
    ffn_norm_g = 1.0 + 0.02 * nrm(ks[11], (DEPTH, D_MODEL), f32)
    w_up = nrm(ks[12], (DEPTH, D_MODEL, 2 * D_FF), f32) * D_MODEL ** -0.5
    conv_w = nrm(ks[13], (DEPTH, CONV_WIDTH, D_FF), f32) * CONV_WIDTH ** -0.5
    conv_b = 0.02 * nrm(ks[14], (DEPTH, D_FF), f32)
    w_down = nrm(ks[15], (DEPTH, D_FF, D_MODEL), f32) * D_FF ** -0.5
    ple_norm_g = 1.0 + 0.02 * nrm(ks[16], (DEPTH, D_MODEL), f32)
    w_ple_gate = nrm(ks[17], (DEPTH, D_MODEL, D_MODEL), f32) * D_MODEL ** -0.5
    w_ple_proj = nrm(ks[18], (DEPTH, PLE_DIM, D_MODEL), f32) * PLE_DIM ** -0.5
    return {"x": x, "p": p, "mix_norm_g": mix_norm_g, "w_in": w_in,
            "mlstm_gate_bias": mlstm_gate_bias, "mlstm_out_g": mlstm_out_g,
            "fox_q_g": fox_q_g, "fox_k_g": fox_k_g, "fox_f_bias": fox_f_bias,
            "w_out": w_out, "ffn_norm_g": ffn_norm_g, "w_up": w_up, "conv_w": conv_w,
            "conv_b": conv_b, "w_down": w_down, "ple_norm_g": ple_norm_g,
            "w_ple_gate": w_ple_gate, "w_ple_proj": w_ple_proj}

def first_block(x, p, mix_norm_g, w_in, mlstm_gate_bias, mlstm_out_g, fox_q_g, fox_k_g, fox_f_bias,
              w_out, ffn_norm_g, w_up, conv_w, conv_b, w_down, ple_norm_g, w_ple_gate, w_ple_proj):
    B, S, _ = x.shape
    f32 = jnp.float32
    split_points = np.cumsum(IN_SIZES)[:-1].tolist()
    for i in range(DEPTH):
        h = rms_norm(x, mix_norm_g[i])
        z = h @ w_in[i]
        mq, mk, mv, mo, mi, mf, fq, fk, fv, ff = jnp.split(z, split_points, axis=-1)

        def heads_a(t):
            return t.reshape(B, S, MLSTM_HEADS, MLSTM_HEAD_DIM).transpose(0, 2, 1, 3).astype(f32)
        ig = (mi + mlstm_gate_bias[i, :MLSTM_HEADS]).astype(f32).transpose(0, 2, 1)
        lf = jax.nn.log_sigmoid((mf + mlstm_gate_bias[i, MLSTM_HEADS:]).astype(f32)).transpose(0, 2, 1)
        ha = mlstm_chunkwise(heads_a(mq), heads_a(mk), heads_a(mv), ig, lf)
        ha = rms_norm(ha.transpose(0, 2, 1, 3), mlstm_out_g[i].reshape(MLSTM_HEADS, MLSTM_HEAD_DIM))
        ha = (ha.reshape(B, S, MLSTM_WIDTH) * jax.nn.sigmoid(mo.astype(f32))).astype(x.dtype)

        qb = rms_norm(fq.reshape(B, S, FOX_HEADS, FOX_HEAD_DIM), fox_q_g[i])
        kb = rms_norm(fk.reshape(B, S, FOX_HEADS, FOX_HEAD_DIM), fox_k_g[i])
        vb = fv.reshape(B, S, FOX_HEADS, FOX_HEAD_DIM)
        logf = jax.nn.log_sigmoid((ff + fox_f_bias[i]).astype(f32))
        hb = forgetting_attention(qb, kb, vb, logf).astype(x.dtype)

        x = x + jnp.concatenate([ha, hb], axis=-1) @ w_out[i]

        h = rms_norm(x, ffn_norm_g[i])
        u = h @ w_up[i]
        a, g = jnp.split(u, 2, axis=-1)
        a = causal_dwconv(a, conv_w[i], conv_b[i])
        x = x + (jax.nn.gelu(a, approximate=False) * g) @ w_down[i]

        gate = jax.nn.sigmoid(rms_norm(x, ple_norm_g[i]) @ w_ple_gate[i])
        x = x + gate * (p[i].astype(x.dtype) @ w_ple_proj[i])
    return x


CHUNK = 64
LEFT_CHUNKS = 8
BAND = LEFT_CHUNKS + 1
N_HEADS = 16
HEAD_DIM = 64
ATTN_WIDTH = N_HEADS * HEAD_DIM
MAX_REL = 128
POOL_WINDOWS = (2, 4, 8, 16)
N_POOL_GROUPS = len(POOL_WINDOWS)
POOL_WIDTH = D_MODEL // 2
POOL_GROUP = POOL_WIDTH // N_POOL_GROUPS
IN_WIDTH = 3 * ATTN_WIDTH + POOL_WIDTH + 2 * D_MODEL
D_FF_2 = ((8 * D_MODEL + 3 * 256 - 1) // (3 * 256)) * 256
NEG_INF = -1e30


def rms_norm_2(x, g):
    xf = x.astype(jnp.float32)
    y = xf * lax.rsqrt(jnp.mean(xf * xf, axis=-1, keepdims=True) + EPS)
    return (y * g.astype(jnp.float32)).astype(x.dtype)

def chunked_rel_attention(q, k, v, rel_bias):
    B, S, _ = q.shape
    nc = S // CHUNK
    qc = q.reshape(B, nc, CHUNK, N_HEADS, HEAD_DIM)
    pad = ((0, 0), (LEFT_CHUNKS * CHUNK, 0), (0, 0))
    kp = jnp.pad(k, pad).reshape(B, nc + LEFT_CHUNKS, CHUNK, N_HEADS, HEAD_DIM)
    vp = jnp.pad(v, pad).reshape(B, nc + LEFT_CHUNKS, CHUNK, N_HEADS, HEAD_DIM)
    band_idx = jnp.arange(nc)[:, None] + jnp.arange(BAND)[None, :]
    kb = kp[:, band_idx].reshape(B, nc, BAND * CHUNK, N_HEADS, HEAD_DIM)
    vb = vp[:, band_idx].reshape(B, nc, BAND * CHUNK, N_HEADS, HEAD_DIM)
    scale = 1.0 / math.sqrt(HEAD_DIM)
    s = jnp.einsum('bnihd,bnjhd->bhnij', qc, kb).astype(jnp.float32) * scale
    i = jnp.arange(CHUNK)
    j = jnp.arange(BAND * CHUNK)
    dist = LEFT_CHUNKS * CHUNK + i[:, None] - j[None, :]
    rel_idx = jnp.clip(dist, -MAX_REL, MAX_REL) + MAX_REL
    bias = rel_bias.astype(jnp.float32)[:, rel_idx]
    key_pos = (jnp.arange(nc)[:, None] - LEFT_CHUNKS) * CHUNK + j[None, :]
    valid = key_pos >= 0
    s = s + bias[None, :, None]
    s = jnp.where(valid[None, None, :, None, :], s, NEG_INF)
    p = jax.nn.softmax(s, axis=-1).astype(v.dtype)
    o = jnp.einsum('bhnij,bnjhd->bnihd', p, vb)
    return o.reshape(B, S, ATTN_WIDTH)

def multiscale_pool(u, pool_w, pool_scale):
    B, S, _ = u.shape
    uf = u.astype(jnp.float32)
    cs = jnp.concatenate([jnp.zeros((B, 1, POOL_WIDTH), jnp.float32),
                          jnp.cumsum(uf, axis=1)], axis=1)
    t = jnp.arange(S)
    outs = []
    for g, w in enumerate(POOL_WINDOWS):
        sl = slice(g * POOL_GROUP, (g + 1) * POOL_GROUP)
        lo = jnp.maximum(t + 1 - w, 0)
        cnt = (t + 1 - lo).astype(jnp.float32)[None, :, None]
        mean = (cs[:, 1:, sl] - cs[:, lo, sl]) / cnt
        outs.append(mean - uf[..., sl])
    d = jnp.stack(outs, axis=2).astype(u.dtype)
    y = jnp.einsum('bsgc,gce->bsge', d, pool_w).reshape(B, S, POOL_WIDTH)
    return y * pool_scale

def swiglu(h, w_gate_up, w_down):
    gu = h @ w_gate_up
    gate, up = gu[..., :D_FF_2], gu[..., D_FF_2:]
    return (jax.nn.silu(gate) * up) @ w_down

def second_inputs(seed: int = 0) -> dict:
    key = jax.random.key(seed)
    ks = jax.random.split(key, 16)
    f32 = jnp.float32

    def nrm(k, shape, fan_in):
        return jax.random.normal(k, shape, f32) * (fan_in ** -0.5)

    def gain(k, shape):
        return 1.0 + 0.02 * jax.random.normal(k, shape, f32)

    return {
        "x": jax.random.normal(ks[0], (BATCH, SEQ, D_MODEL), f32),
        "norm_mix": gain(ks[1], (DEPTH, D_MODEL)),
        "w_in": nrm(ks[2], (DEPTH, D_MODEL, IN_WIDTH), D_MODEL),
        "rel_bias": 0.1 * jax.random.normal(ks[3], (DEPTH, N_HEADS, 2 * MAX_REL + 1), f32),
        "pool_w": nrm(ks[4], (DEPTH, N_POOL_GROUPS, POOL_GROUP, POOL_GROUP), POOL_GROUP),
        "pool_scale": gain(ks[5], (DEPTH, POOL_WIDTH)),
        "w_branch_a": nrm(ks[6], (DEPTH, ATTN_WIDTH, D_MODEL), ATTN_WIDTH),
        "w_branch_b": nrm(ks[7], (DEPTH, POOL_WIDTH, D_MODEL), POOL_WIDTH),
        "w_out": nrm(ks[8], (DEPTH, D_MODEL, D_MODEL), D_MODEL),
        "norm_ffn": gain(ks[9], (DEPTH, D_MODEL)),
        "w_gate_up": nrm(ks[10], (DEPTH, D_MODEL, 2 * D_FF_2), D_MODEL),
        "w_down": nrm(ks[11], (DEPTH, D_FF_2, D_MODEL), D_FF_2),
        "norm_final": gain(ks[12], (D_MODEL,)),
    }

def second_block(x, norm_mix, w_in, rel_bias, pool_w, pool_scale, w_branch_a, w_branch_b,
              w_out, norm_ffn, w_gate_up, w_down, norm_final):
    a0 = 3 * ATTN_WIDTH
    a1 = a0 + POOL_WIDTH
    a2 = a1 + D_MODEL
    for l in range(DEPTH):
        h = rms_norm_2(x, norm_mix[l])
        z = h @ w_in[l]
        q = z[..., :ATTN_WIDTH]
        k = z[..., ATTN_WIDTH:2 * ATTN_WIDTH]
        v = z[..., 2 * ATTN_WIDTH:a0]
        u = z[..., a0:a1]
        gate_a = jax.nn.sigmoid(z[..., a1:a2])
        gate_b = jax.nn.sigmoid(z[..., a2:])
        y_a = chunked_rel_attention(q, k, v, rel_bias[l])
        y_b = multiscale_pool(u, pool_w[l], pool_scale[l])
        merged = gate_a * (y_a @ w_branch_a[l]) + gate_b * (y_b @ w_branch_b[l])
        x = x + merged @ w_out[l]
        x = x + swiglu(rms_norm_2(x, norm_ffn[l]), w_gate_up[l], w_down[l])
    return rms_norm_2(x, norm_final)


def setup_inputs(seed=0):
    out = dict(first_inputs(seed))
    for name, value in second_inputs(seed + 1).items():
        if name != "x":
            out[name + "_2"] = value
    return out


def reference(
    x, p, mix_norm_g, w_in, mlstm_gate_bias, mlstm_out_g, fox_q_g, fox_k_g, fox_f_bias, w_out,
    ffn_norm_g, w_up, conv_w, conv_b, w_down, ple_norm_g, w_ple_gate, w_ple_proj, norm_mix_2,
    w_in_2, rel_bias_2, pool_w_2, pool_scale_2, w_branch_a_2, w_branch_b_2, w_out_2, norm_ffn_2,
    w_gate_up_2, w_down_2, norm_final_2,
):
    x = first_block(
        x, p, mix_norm_g, w_in, mlstm_gate_bias, mlstm_out_g, fox_q_g, fox_k_g, fox_f_bias,
        w_out, ffn_norm_g, w_up, conv_w, conv_b, w_down, ple_norm_g, w_ple_gate, w_ple_proj,
    )
    return second_block(
        x, norm_mix_2, w_in_2, rel_bias_2, pool_w_2, pool_scale_2, w_branch_a_2, w_branch_b_2,
        w_out_2, norm_ffn_2, w_gate_up_2, w_down_2, norm_final_2,
    )


_drawn_inputs = setup_inputs


def setup_inputs(seed=0):
    import zlib

    import numpy as np

    out = dict(_drawn_inputs(seed))
    spreads = {}
    factors = {'mlstm_out_g': 6.953,
     'fox_q_g': 8.0,
     'fox_k_g': 8.0,
     'ffn_norm_g': 3.861,
     'conv_b': 5.473,
     'ple_norm_g': 64.0,
     'norm_mix_2': 7.353,
     'rel_bias_2': 30.205,
     'pool_scale_2': 21.942,
     'norm_ffn_2': 22.087,
     'norm_final_2': 7.413}
    for name, (base, spread) in spreads.items():
        noise = np.random.default_rng([zlib.crc32(name.encode()), seed]).standard_normal(out[name].shape)
        drawn = base * np.exp(spread * noise) if base else spread * noise
        out[name] = __import__('jax').numpy.asarray(drawn.astype(out[name].dtype))
    for name, factor in factors.items():
        out[name] = (out[name] * factor).astype(out[name].dtype)
    return out
```

```python
from contextlib import ExitStack

import concourse.bass as bass
from concourse import mybir

F32 = mybir.dt.float32
F32R = mybir.dt.float32r
ALU = mybir.AluOpType
ACT = mybir.ActivationFunctionType
AX = mybir.AxisListType
ds = bass.ds

P = 128
SLOTS = 4
KS = 2
W = 512
NEG = -1.0e30
EPS = 1.0e-6


def sandwich_kernel(nc, A, out, bias_scratch):
    S, D = A["x"].shape[1:]
    T = S // P
    KD = D // P
    NB = D // W
    MH, FH = A["mlstm_gate_bias"].shape[1] // 2, A["fox_f_bias"].shape[1]
    MW = A["mlstm_out_g"].shape[1]
    MD = MW // MH
    FD = A["fox_q_g"].shape[1]
    FF = A["w_down"].shape[1]
    KF = FF // P
    PLE = A["p"].shape[3]
    AH, RB = A["rel_bias_2"].shape[1:]
    G = A["pool_w_2"].shape[1]
    PG = A["pool_w_2"].shape[2]
    AW = A["w_branch_a_2"].shape[1]
    AD = AW // AH
    MAXREL = (RB - 1) // 2
    EXT = 3 * P
    POOL_WINDOWS = [2 ** (g + 1) for g in range(G)]
    NG = 2 * MH + FH
    assert (S, D, MH, MD, FH, FD) == (256, 2048, 4, 256, 8, 128) and FF % W == 0 and KF % KS == 0
    assert PLE == KS * P and AD == 64 and MAXREL == P and PG == 2 * P and G * PG == D // 2

    def rows(w, c0, k0, n):
        return w[k0 * P:(k0 + n) * P, ds(c0, W)].rearrange("(k p) c -> p k c", p=P)

    w_in, w_out, w_up, w_down = A["w_in"][0], A["w_out"][0], A["w_up"][0], A["w_down"][0]
    w_gate, w_proj = A["w_ple_gate"][0], A["w_ple_proj"][0]
    w_in2, w_a2, w_b2, w_out2 = A["w_in_2"][0], A["w_branch_a_2"][0], A["w_branch_b_2"][0], A["w_out_2"][0]
    w_gu2, w_dn2 = A["w_gate_up_2"][0], A["w_down_2"][0]
    FOX0 = 4 * MW + 2 * MH

    def mlstm_rows(h, which, k):
        v = w_in[k * P:(k + 1) * P, 2 * MW * which:2 * MW * (which + 1)]
        return v.rearrange("p (j h c) -> p h j c", j=2, h=MH)[:, ds(h, 1)].rearrange("p o j c -> p (o j) c")

    def fox_rows(h, k):
        v = w_in[k * P:(k + 1) * P, FOX0:FOX0 + 3 * FH * FD]
        return v.rearrange("p (j h c) -> p h j c", j=3, h=FH)[:, ds(h, 1)].rearrange("p o j c -> p (o j) c")

    def rel_rows(b, k):
        v = w_in2[k * P:(k + 1) * P, 0:4 * AW]
        return v.rearrange("p (j b c) -> p b j c", j=4, c=P)[:, ds(b, 1)].rearrange("p o j c -> p (o j) c")

    PHASES = {
        "init": (0, 0, 1, (NB, NB, 3, 2)),
        "mlstm": (MH, 16, 2, (2 * MH, 3 * MH, MH, MH)),
        "fox": (FH // 2, 16, 2, (FH, FH, FH, 2 * FH)),
        "out": (NB // 2, 16, 1, (NB, NB, 0, 0)),
        "up": (FF // W, 16, 1, (FF // W,) * 4),
        "down": (NB // 2, KF, 1, (NB, NB, 1, 0)),
        "proj": (NB // 2, 2, 1, (0, 0, 0, 0)),
        "gate": (NB // 2, 16, 1, (NB, NB, 0, 0)),
        "rel": (AH // 4, 16, 2, (AH, AH, AH, AH // 2 + G)),
        "mix": (2 * NB, 12, 1, (NB, NB, 0, 0)),
        "out2": (NB // 2, 16, 1, (NB, NB, 0, 0)),
        "up2": (FF // W, 16, 1, (FF // W,) * 4),
        "down2": (NB // 2, KF, 1, (0, 0, 0, 0)),
    }
    STAGE0, PAIR0, LAND0, DMAS = {}, {}, {}, {}
    USE0 = [{}, {}, {}, {}]
    stage = pair = land = 0
    use = [0, 0, 0, 0]
    for name, (pairs, stages, dmas, uses) in PHASES.items():
        STAGE0[name], PAIR0[name], LAND0[name], DMAS[name] = stage, pair, land, dmas
        for b in range(4):
            USE0[b][name] = use[b]
            use[b] += uses[b]
        stage, pair = stage + pairs * stages, pair + pairs
        land += 16 * dmas * pairs * stages // SLOTS
    T1, T2, X1, X2 = range(4)

    class Window:
        def __init__(self, phase, i, first, stages, par, width=W, pair=None):
            self.i, self.first, self.n, self.par, self.width = i, first, stages, par, width
            self.dmas = DMAS[phase]
            per = PHASES[phase][1]
            if phase == "mix":
                per = 2 * per
            self.per, self.stage0, self.land0 = per, STAGE0[phase], LAND0[phase]
            self.block = PAIR0[phase] + (i if pair is None else pair)

        def slot(self, j):
            return (self.first + j) % SLOTS

        def stages_to(self, j):
            return self.i * self.per + (self.stage0 + self.first + j + 1)

        def landed(self, j):
            per_turn = 16 * self.dmas
            return self.i * (per_turn * self.per // SLOTS) + (self.land0 + per_turn * ((self.first + j) // SLOTS + 1))

        def end(self):
            return self.stages_to(self.n - 1)

    def pair_windows(phase, i, width=W):
        n = PHASES[phase][1] // 2
        return [Window(phase, i, 0, n, 0, width), Window(phase, i, n, n, 1, width)]

    mlstm_w = lambda h: pair_windows("mlstm", h)
    fox_w = lambda i: pair_windows("fox", i, 3 * FD)
    up_w = lambda ph, i: pair_windows(ph, i)

    def mix_windows(n):
        return [Window("mix", n, 0, 8, 0, pair=2 * n), Window("mix", n, 8, 8, 1, pair=2 * n),
                Window("mix", n, 16, 4, 0, pair=2 * n + 1), Window("mix", n, 20, 4, 1, pair=2 * n + 1)]

    def proj_windows():
        return [Window("proj", 0, n, 1, n % 2, pair=n // 2) for n in range(NB)]

    RES0 = {"init": 0, "out": NB, "down": 2 * NB, "gate": 3 * NB, "mix": 4 * NB, "out2": 5 * NB}
    NORM = {"init": 0, "out": 1, "down": 2, "gate": 3, "out2": 4, "down2": 5}
    FFN0 = {"up": 0, "up2": FF // W}

    with ExitStack() as ctx:
        def sb(name, shape, dt=F32, where=ctx):
            return where.enter_context(nc.sbuf_tensor(name, shape, dt))

        def sem(name):
            return ctx.enter_context(nc.semaphore(name))

        raw = sb("raw", [P, SLOTS, KS, W])
        whi = sb("whi", [P, SLOTS, KS, W], F32R)
        wlo = sb("wlo", [P, SLOTS, KS, W], F32R)
        xres = sb("xres", [P, T, D])
        with ExitStack() as final:
            gfin = sb("gfin", [P, D], F32, final)
        xt_hi = sb("xt_hi", [P, KD, S], F32R)
        xt_lo = sb("xt_lo", [P, KD, S], F32R)
        sq_out = sb("sq_out", [P, W])
        ident = sb("ident", [P, P])
        anti = sb("anti", [P, P])
        ones = sb("ones", [P, S])
        gains = sb("gains", [P, 5 * KD + 2 * (MW // P) + 2])
        convs = sb("convs", [P, 4 * KF])
        sumsq = sb("sumsq", [P, 6, T, NB])
        meansq = sb("meansq", [P, 6, T])
        rstd = sb("rstd", [P, 6, T])
        half = sb("half", [P, 4])
        negs = sb("negs", [P, P])
        small = sb("small", [P, 64])
        M_MS, M_RS, M_COMB, M_DEN, M_RDEN = (small[:, 2 * n:2 * n + 2] for n in range(5))
        M_ND = small[:, 10:12]
        F_SS, F_RS = small[:, 12:16], small[:, 16:20]
        F_MX, F_NMX, F_SUM, F_RINV = (small[:, 20 + 2 * n:22 + 2 * n] for n in range(4))
        A_MX, A_NMX, A_SUM, A_RINV = (small[:, 28 + 4 * n:32 + 4 * n] for n in range(4))
        g_mix, g_ffn, g_ple, g_mix2, g_ffn2 = (KD * n for n in range(5))
        g_mlstm = 5 * KD
        g_pool = g_mlstm + MW // P
        g_fq = g_pool + G * PG // P
        g_fk = g_fq + 1
        NGAIN = g_fk + 1

        def group(tensors, where):
            return [sb(name, shape, dt, where) for name, shape, dt in tensors]

        with ExitStack() as start:
            gain_rows, conv_rows, bias_ext = group([
                ("gain_rows", [P, P], F32), ("conv_rows", [2 * KF, 2, P], F32), ("bias_ext", [AH, EXT], F32)], start)
        with ExitStack() as ple:
            p_s, pt_hi, pt_lo = group([
                ("p_s", [P, T, PLE], F32), ("pt_hi", [P, KS, S], F32R), ("pt_lo", [P, KS, S], F32R)], ple)
        with ExitStack() as rel:
            band, btile = group([("band", [P, G, S + P], F32), ("btile", [P, 2, 2, 2, P], F32)], rel)
        with ExitStack() as mix:
            sgb, merged, sga = group([
                ("sgb", [P, T, W], F32), ("merged", [P, T, W], F32), ("sga", [P, T, W], F32)], mix)
        a_s, g_s, hid = group([("a_s", [P, T, W], F32), ("g_s", [P, T, W], F32), ("hid", [P, 4, S], F32)], ctx)

        with ExitStack() as hidden:
            ht_hi, ht_lo = group([("ht_hi", [P, KF, S], F32R), ("ht_lo", [P, KF, S], F32R)], hidden)
        with ExitStack() as second:
            zt_hi, zt_lo = group([("zt_hi", [P, KD, S], F32R), ("zt_lo", [P, KD, S], F32R)], second)
            with ExitStack() as embed:
                pp, sg_s = group([("pp", [P, T, D], F32), ("sg_s", [P, T, W], F32)], embed)
            mt_hi, mt_lo, s_s, rqt_s, rkt_s, rp_s, rpt_s, dt_s, pw = group([
                ("mt_hi", [P, KD, S], F32R), ("mt_lo", [P, KD, S], F32R),
                ("s_s", [P, 2, T, W], F32), ("rqt_s", [P, S], F32), ("rkt_s", [P, S], F32),
                ("rp_s", [P, 2, S + P], F32), ("rpt_s", [P, 2, S + P], F32),
                ("dt_s", [P, 2, S], F32), ("pw", [P, 2, PG], F32)], second)
        (yt_hi, yt_lo, wg_raw, wg_hi, wg_lo, bias_bc, gl, lsx, crow, cols, em, diag_m, diag_f, mask_m, mask_f,
         qk_s, v_s, so_s, qt_s, kt_s, dw_s, pt_s, y_s, f_s, fqk_s, fsq_s, fqt_s, fkt_s, fg_s, fp_s, fpt_s) = group([
            ("yt_hi", [P, KD, S], F32R), ("yt_lo", [P, KD, S], F32R),
            ("wg_raw", [P, KD, NG], F32), ("wg_hi", [P, KD, NG], F32R), ("wg_lo", [P, KD, NG], F32R),
            ("bias_bc", [P, NG], F32), ("gl", [P, T, NG], F32), ("lsx", [P, 8, T, MH + FH], F32),
            ("crow", [8, 6, S], F32), ("cols", [P, T, NG], F32), ("em", [P, T, MH], F32),
            ("diag_m", [MH, MH, S], F32), ("diag_f", [FH, FH, S], F32),
            ("mask_m", [P, S + P], F32), ("mask_f", [P, S + P], F32),
            ("qk_s", [P, T, 2 * MD], F32), ("v_s", [P, T, MD], F32), ("so_s", [P, T, MD], F32),
            ("qt_s", [P, 2, S], F32), ("kt_s", [P, 2, S], F32), ("dw_s", [P, S + P], F32),
            ("pt_s", [P, S + P], F32), ("y_s", [P, T, MD], F32),
            ("f_s", [P, 2, T, 3 * FD], F32), ("fqk_s", [P, T, 2 * FD], F32), ("fsq_s", [P, T, 2 * FD], F32),
            ("fqt_s", [P, S], F32), ("fkt_s", [P, S], F32), ("fg_s", [P, S + P], F32),
            ("fp_s", [P, S + P], F32), ("fpt_s", [P, S + P], F32)], ctx)

        acc = [[ctx.enter_context(nc.psum_tensor(f"acc{par}{t}", [P, W], F32)) for t in range(T)] for par in range(2)]
        bank = [ctx.enter_context(nc.psum_tensor(name, [P, W], F32)) for name in ("T1", "T2", "X1", "X2")]

        raw_landed = [sem(f"raw_landed{s}") for s in range(SLOTS)]
        hi_made = sem("hi_made")
        lo_made = sem("lo_made")
        stage_used = sem("stage_used")
        acc_read = [sem(f"acc_read{par}") for par in range(2)]
        bank_read = [sem(f"bank_read{b}") for b in range(4)]
        slot_waited = sem("slot_waited")
        x_landed = [sem(f"x_landed{n}") for n in range(NB)]
        square_done = sem("square_done")
        meansq_done = sem("meansq_done")
        meansq_eps = sem("meansq_eps")
        rstd_done = sem("rstd_done")
        res_turned = sem("res_turned")
        split_hi = sem("split_hi")
        gains_landed, convs_landed, gate_w_landed, bias_landed = (sem(n) for n in (
            "gains_landed", "convs_landed", "gate_w_landed", "bias_landed"))
        const_made, gain_made = sem("const_made"), sem("gain_made")
        const_cleared = sem("const_cleared")
        band_set, band_made = sem("band_set"), sem("band_made")
        N_CONST = 6
        N_LOGIT = 17
        gains_turned = sem("gains_turned")
        gate_w_hi, gate_w_lo = sem("gate_w_hi"), sem("gate_w_lo")
        logits_made, logit_step, logit_exp = sem("logits_made"), sem("logit_step"), sem("logit_exp")
        rows_turned, row_step, cols_turned = sem("rows_turned"), sem("row_step"), sem("cols_turned")
        em_made, diag_made = sem("em_made"), sem("diag_made")
        ext_landed, ext_made, ext_stored = sem("ext_landed"), sem("ext_made"), sem("ext_stored")
        m_turned, m_kt, m_scored, m_decay, m_weight, m_probs = (sem(n) for n in (
            "m_turned", "m_kt", "m_scored", "m_decay", "m_weight", "m_probs"))
        m_qt, m_so, m_num, m_nd, m_dmax, m_den, m_rden, m_sq, m_eps, m_rs, m_comb, m_y, m_yturned, m_yhi = (sem(n) for n in (
            "m_qt", "m_so", "m_num", "m_nd", "m_dmax", "m_den", "m_rden", "m_sq", "m_eps", "m_rs", "m_comb", "m_y",
            "m_yturned", "m_yhi"))
        f_sq, f_ss, f_eps, f_rs, f_norm, f_turned, f_qt, f_scored, f_bias, f_logit, f_max, f_nmax, f_exp, f_rinv, f_probs, \
            f_pturned, f_out, f_yhi = (sem(n) for n in (
                "f_sq", "f_ss", "f_eps", "f_rs", "f_norm", "f_turned", "f_qt", "f_scored", "f_bias", "f_logit", "f_max",
                "f_nmax", "f_exp", "f_rinv", "f_probs", "f_pturned", "f_out", "f_yhi"))
        a_turned, g_turned, conv_step, hid_act, hid_hi, hid_lo = (sem(n) for n in (
            "a_turned", "g_turned", "conv_step", "hid_act", "hid_hi", "hid_lo"))
        p_landed, p_turned, p_hi, pp_made, gated, res_done = (sem(n) for n in (
            "p_landed", "p_turned", "p_hi", "pp_made", "gated", "res_done"))
        btile_landed, btile_made, pw_landed = sem("btile_landed"), sem("btile_made"), sem("pw_landed")
        r_turned, r_qt, r_pooled, r_scored, r_max, r_nmax, r_exp, r_rinv, r_probs, r_pturned, r_out, r_yhi, \
            y_pool, y_phi, r_vused = (sem(n) for n in (
                "r_turned", "r_qt", "r_pooled", "r_scored", "r_max", "r_nmax", "r_exp", "r_rinv", "r_probs", "r_pturned",
                "r_out", "r_yhi", "y_pool", "y_phi", "r_vused"))
        b_scaled, merged_made = sem("b_scaled"), sem("merged_made")
        gfin_landed, out_made, stored = sem("gfin_landed"), sem("out_made"), sem("stored")

        block = ctx.enter_context(nc.Block())

        def reached(eng, semaphore, count):
            if isinstance(count, int) and count <= 0:
                return
            eng.wait_ge(semaphore, count)

        @block.sync
        def _(sp):
            for n in range(NB):
                sp.dma_start(xres[:, :, n * W:(n + 1) * W],
                             A["x"][0][:, n * W:(n + 1) * W].rearrange("(t p) c -> p t c", p=P)).then_inc(x_landed[n], 16)

            def load(w, view, wait_apart=False):
                for j in range(w.n):
                    s = w.slot(j)
                    reached(sp, lo_made, w.stages_to(j) - SLOTS)
                    if wait_apart:
                        sp.sem_inc(slot_waited, 1)
                    for ks, src in view(j):
                        sp.dma_start(raw[:, s, ks, 0:w.width], src).then_inc(raw_landed[s], 16)

            def settled(v):
                return v if isinstance(v, int) else sp.snap(v)

            def plain(weights, c0):
                return lambda j: [(slice(0, KS), rows(weights, c0, KS * j, KS))]

            def by_ktile(f):
                return lambda j: [(k, f(KS * j + k)) for k in range(KS)]

            def mlstm_loads(h):
                h = settled(h)
                a, b = pair_windows("mlstm", h)
                load(a, by_ktile(lambda k: mlstm_rows(h, 0, k)))
                load(b, by_ktile(lambda k: mlstm_rows(h, 1, k)))

            def fox_loads(i):
                for par, w in enumerate(fox_w(i)):
                    load(w, by_ktile(lambda k: fox_rows(2 * i + par, k)))

            def ffn_loads(phase, weights, i):
                a, b = pair_windows(phase, i)
                load(a, plain(weights, i * W))
                load(b, plain(weights, i * W + FF))

            def pair_loads(phase, weights, i):
                for par, w in enumerate(pair_windows(phase, i)):
                    load(w, plain(weights, (2 * i + par) * W))

            def rel_loads(i):
                for par, w in enumerate(pair_windows("rel", i)):
                    load(w, by_ktile(lambda k: rel_rows(2 * i + par, k)))

            def mix_loads(n):
                ga, gb, ba, bb = mix_windows(n)
                load(ga, plain(w_in2, n * W + 4 * AW))
                load(gb, plain(w_in2, n * W + 4 * AW + D))
                load(ba, plain(w_a2, n * W), wait_apart=True)
                load(bb, plain(w_b2, n * W))

            mlstm_loads(0)
            with sp.Fori(1, MH) as h:
                mlstm_loads(h)
            with sp.Fori(0, FH // 2) as i:
                fox_loads(i)
            with sp.Fori(0, NB // 2) as i:
                pair_loads("out", w_out, i)
            with sp.Fori(0, FF // W) as i:
                ffn_loads("up", w_up, i)
            with sp.Fori(0, NB // 2) as i:
                pair_loads("down", w_down, i)
            for n, w in enumerate(proj_windows()):
                load(w, plain(w_proj, n * W))
            with sp.Fori(0, NB // 2) as i:
                pair_loads("gate", w_gate, i)
            with sp.Fori(0, AH // 4) as i:
                rel_loads(i)
            mix_loads(0)
            with sp.Fori(1, NB) as n:
                mix_loads(n)
            with sp.Fori(0, NB // 2) as i:
                pair_loads("out2", w_out2, i)
            with sp.Fori(0, FF // W) as i:
                ffn_loads("up2", w_gu2, i)
            with sp.Fori(0, NB // 2) as i:
                pair_loads("down2", w_dn2, i)
            for n in range(NB):
                sp.wait_ge(out_made, T * (n + 1))
                sp.dma_start(out[0][:, n * W:(n + 1) * W].rearrange("(t p) c -> p t c", p=P),
                             xres[:, :, n * W:(n + 1) * W]).then_inc(stored, 16)
            sp.wait_ge(stored, 16 * NB)

        @block.scalar
        def _(act):
            def hi(w, after={}):
                for j in range(w.n):
                    s = w.slot(j)
                    act.wait_ge(raw_landed[s], w.landed(j))
                    reached(act, stage_used, w.stages_to(j) - SLOTS)
                    act.activation(whi[:, s, :, 0:w.width], raw[:, s, :, 0:w.width], ACT.Copy).then_inc(hi_made, 1)
                    for piece in after.get(j, []):
                        piece()

            def square(phase, n, ready, count):
                norm = NORM[phase]
                act.wait_ge(ready, count)
                for t in range(T):
                    reached(act, square_done, T * (NB * norm + n) + t)
                    act.activation(sq_out[:], xres[:, t, n * W:(n + 1) * W], ACT.Square,
                                   accum_out=sumsq[:, norm, t, n:n + 1]).then_inc(square_done, 1)

            def split(phase, n, dst, gain):
                r = RES0[phase] + n
                for kk in range(4):
                    act.wait_ge(res_turned, 2 * r + 1 + kk // 2)
                    k = 4 * n + kk
                    scale = 1.0 if gain is None else gains[:, gain + k:gain + k + 1]
                    act.activation(dst[:, ds(k, 1), :].rearrange("p o c -> p (o c)"), bank[kk // 2][:, (kk % 2) * S:(kk % 2 + 1) * S], ACT.Copy,
                                   scale=scale).then_inc(split_hi, 1)

            col = 0
            for name, nrows in (("mix_norm_g", KD), ("ffn_norm_g", KD), ("ple_norm_g", KD), ("norm_mix_2", KD),
                                ("norm_ffn_2", KD), ("mlstm_out_g", MW // P), ("pool_scale_2", G * PG // P),
                                ("fox_q_g", 1), ("fox_k_g", 1)):
                act.dma_start(gain_rows[col:col + nrows, :], A[name].rearrange("o (k p) -> (o k) p", p=P)).then_inc(gains_landed, 16)
                col += nrows
            for tap in range(3):
                act.dma_start(conv_rows[KF * (tap % 2):KF * (tap % 2 + 1), tap // 2, :],
                              A["conv_w"][0][tap:tap + 1, :].rearrange("o (k p) -> (o k) p", p=P)).then_inc(convs_landed, 16)
            act.dma_start(conv_rows[KF:2 * KF, 1, :], A["conv_b"].rearrange("o (k p) -> (o k) p", p=P)).then_inc(convs_landed, 16)
            w_in_k = w_in.rearrange("(k p) c -> p k c", p=P)
            act.dma_start(wg_raw[:, :, 0:2 * MH], w_in_k[:, :, 4 * MW:FOX0]).then_inc(gate_w_landed, 16)
            act.dma_start(wg_raw[:, :, 2 * MH:NG], w_in_k[:, :, FOX0 + 3 * FH * FD:]).then_inc(gate_w_landed, 16)
            act.dma_start(bias_bc[:, 0:2 * MH], A["mlstm_gate_bias"].partition_broadcast(P).rearrange("p o c -> p (o c)")).then_inc(bias_landed, 16)
            act.dma_start(bias_bc[:, 2 * MH:NG], A["fox_f_bias"].partition_broadcast(P).rearrange("p o c -> p (o c)")).then_inc(bias_landed, 16)

            act.wait_ge(gains_turned, 1)
            act.activation(gains[:, 0:NGAIN], bank[X1][:, 0:NGAIN], ACT.Copy).then_inc(gain_made, 1)
            act.activation(convs[:, :], bank[X1][:, P:P + 4 * KF], ACT.Copy).then_inc(bank_read[X1], 1)
            act.wait_ge(gain_made, 1)
            for n in range(NB):
                split("init", n, xt_hi, g_mix)
            for n in range(NB):
                square("init", n, x_landed[n], 16)
            act.wait_ge(gate_w_landed, 32)
            act.activation(wg_hi[:], wg_raw[:], ACT.Copy).then_inc(gate_w_hi, 1)

            def logits_exp():
                act.wait_ge(logit_step, 2)
                act.activation(lsx[:, 2], lsx[:, 1], ACT.Exp, scale=-1.0).then_inc(logit_exp, 1)

            def em_exp():
                act.wait_ge(bank_read[X1], USE0[X1]["init"] + 3)
                act.activation(em[:, :, :], cols[:, :, MH:2 * MH], ACT.Exp, scale=-1.0).then_inc(em_made, 1)

            def m_evac_qk(w):
                act.wait_ge(rstd_done, 1)
                act.wait_ge(stage_used, w.end())
                act.activation(qk_s[:, 0, :], acc[0][0][:], ACT.Copy, scale=rstd[:, 0, 0:1]).then_inc(acc_read[0], 1)

            def m_copy_qt(h):
                act.wait_ge(m_turned, 2 * h + 1)
                act.activation(qt_s[:, :, :].rearrange("p a b -> p (a b)"), bank[T1][:], ACT.Copy).then_inc(bank_read[T1], 1)

            def m_exp(h):
                act.wait_ge(bank_read[X2], USE0[X2]["mlstm"] + h + 1)
                act.activation(dw_s[:, 0:S], dw_s[:, 0:S], ACT.Exp, bias=cols[:, 0, ds(h, 1)]).then_inc(m_weight, 1)
                act.activation(dw_s[:, S:S + P], dw_s[:, S:S + P], ACT.Exp, bias=cols[:, 1, ds(h, 1)]).then_inc(m_weight, 1)

            def m_gate(h, w):
                act.wait_ge(stage_used, w.end())
                for t in range(T):
                    act.activation(so_s[:, t, :], acc[1][t][:, MD:2 * MD], ACT.Sigmoid,
                                   scale=rstd[:, 0, t:t + 1]).then_inc(m_so, 1)

            def m_squares(h):
                act.wait_ge(m_rden, h + 1)
                for t in range(T):
                    reached(act, m_sq, T * h + t)
                    act.activation(sq_out[:, 0:MD], bank[T1][:, t * MD:(t + 1) * MD], ACT.Square,
                                   scale=M_RDEN[:, t:t + 1], accum_out=M_MS[:, t:t + 1]).then_inc(m_sq, 1)

            def m_split(h):
                act.wait_ge(m_yturned, h + 1)
                for d in range(2):
                    act.activation(yt_hi[:, ds(2 * h + d, 1), :].rearrange("p o c -> p (o c)"), bank[T2][:, d * S:(d + 1) * S], ACT.Copy,
                                   scale=gains[:, ds(2 * h + (g_mlstm + d), 1)]).then_inc(m_yhi, 1)

            def mlstm(h, first, early={}):
                a, b = pair_windows("mlstm", h)
                prev = None if first else h - 1
                after_a = dict(early)
                after_b = {3: [lambda: m_evac_qk(a)], 4: [lambda: m_copy_qt(h)], 7: [lambda: m_exp(h)]}
                if not first:
                    pa, pb = pair_windows("mlstm", prev)
                    after_a = {3: [lambda: m_gate(prev, pb)], 6: [lambda: m_squares(prev)]}
                    after_b[1] = [lambda: m_split(prev)]
                hi(a, after_a)
                hi(b, after_b)

            mlstm(0, True, {2: [logits_exp], 7: [em_exp]})
            with act.Fori(1, MH) as h:
                mlstm(h, False)

            def f_evac(b, w):
                act.wait_ge(stage_used, w.end())
                act.activation(f_s[:, w.par, 0, :], acc[w.par][0][:, 0:3 * FD], ACT.Copy,
                               scale=rstd[:, 0, 0:1]).then_inc(acc_read[w.par], 1)

            def f_copy_qt(b):
                act.wait_ge(f_turned, b + 1)
                act.activation(fqt_s[:], bank[T1][:, 0:S], ACT.Copy, scale=gains[:, g_fq:g_fq + 1]).then_inc(f_qt, 1)
                act.activation(fkt_s[:], bank[T1][:, S:2 * S], ACT.Copy, scale=gains[:, g_fk:g_fk + 1]).then_inc(bank_read[T1], 1)

            def f_softmax(b):
                act.wait_ge(f_nmax, b + 1)
                for t, cols_ in ((0, slice(0, P)), (1, slice(P, P + S))):
                    act.activation(fp_s[:, cols_], fg_s[:, cols_], ACT.Exp, bias=F_NMX[:, t:t + 1],
                                   accum_out=F_SUM[:, t:t + 1]).then_inc(f_exp, 1)

            def f_copy_pt(b):
                act.wait_ge(f_pturned, b + 1)
                act.activation(fpt_s[:], bank[T2][:, 0:S + P], ACT.Copy).then_inc(bank_read[T2], 1)

            def f_split(b):
                act.wait_ge(f_out, b + 1)
                act.activation(yt_hi[:, ds(b + MW // P, 1), :].rearrange("p o c -> p (o c)"), bank[X2][:, 0:S], ACT.Copy).then_inc(f_yhi, 1)

            def fox_pieces(b, w, last=None):
                after = {3: [lambda: f_evac(b, w)], 5: [lambda: f_copy_qt(b)], 7: [lambda: f_softmax(b)]}
                if last is not None:
                    after[1] = [lambda: f_copy_pt(last)]
                    after[4] = [lambda: f_split(last)]
                return after

            _, m_last = pair_windows("mlstm", MH - 1)
            w0, w1 = fox_w(0)
            hi(w0, {3: [lambda: m_gate(MH - 1, m_last)], 6: [lambda: m_squares(MH - 1)]})
            pieces = fox_pieces(0, w0)
            pieces[1] = [lambda: m_split(MH - 1)]
            hi(w1, pieces)
            with act.Fori(1, FH // 2) as i:
                _, before = fox_w(i - 1)
                w0, w1 = fox_w(i)
                hi(w0, fox_pieces(2 * i - 1, before, 2 * i - 2))
                hi(w1, fox_pieces(2 * i, w0, 2 * i - 1))

            def residual(phase, n, w, dst, gain, at=(3, 5)):
                return {at[0]: [lambda: square(phase, n, acc_read[w.par], 2 * w.block + 2)],
                        at[1]: [lambda: split(phase, n, dst, gain)]}

            ws = [w for i in range(NB // 2) for w in pair_windows("out", i)]
            _, before = fox_w(FH // 2 - 1)
            hi(ws[0], {1: [lambda: f_copy_pt(FH - 2)], 3: [lambda: f_evac(FH - 1, before)],
                       4: [lambda: f_split(FH - 2), lambda: f_copy_qt(FH - 1)], 5: [lambda: f_softmax(FH - 1)],
                       6: [lambda: f_copy_pt(FH - 1)], 7: [lambda: f_split(FH - 1)]})
            for n in range(1, NB):
                hi(ws[n], residual("out", n - 1, ws[n - 1], xt_hi, g_ffn))
            before = ws[-1]

            def ffn_evac(phase, w):
                act.wait_ge(rstd_done, NORM["out" if phase == "up" else "out2"] + 1)
                act.wait_ge(stage_used, w.end())
                for t in range(T):
                    norm = NORM["out" if phase == "up" else "out2"]
                    act.activation(a_s[:, t, :], acc[0][t][:], ACT.Copy, scale=rstd[:, norm, t:t + 1]).then_inc(acc_read[0], 1)

            def ffn_act(phase, i):
                f = FFN0[phase] + i
                if phase == "up":
                    act.wait_ge(bank_read[T2], USE0[T2][phase] + i + 1)
                    act.activation(hid[:], hid[:], ACT.Gelu).then_inc(hid_act, 1)
                else:
                    reached(act, hid_lo, f)
                    for half_ in range(2):
                        act.wait_ge(a_turned, 2 * f + 1 + half_)
                        act.activation(hid[:, 2 * half_:2 * half_ + 2, :].rearrange("p a b -> p (a b)"), bank[T1 + half_][:],
                                       ACT.Silu).then_inc(bank_read[T1 + half_], 1)

            def ffn_split(phase, i):
                act.wait_ge(bank_read[X2], USE0[X2][phase] + i + 1)
                act.activation(ht_hi[:, ds(4 * i, 4), :], hid[:], ACT.Copy).then_inc(hid_hi, 1)

            def ffn_tail(phase, i):
                return {1: [lambda: ffn_act(phase, i)], 6: [lambda: ffn_split(phase, i)]}

            def ffn(phase, i, pieces):
                a, g = pair_windows(phase, i)
                hi(a, pieces)
                hi(g, {3: [lambda: ffn_evac(phase, a)]})

            ffn("up", 0, residual("out", NB - 1, before, xt_hi, g_ffn))
            with act.Fori(1, FF // W) as i:
                ffn("up", i, ffn_tail("up", i - 1))
            ws = [w for i in range(NB // 2) for w in pair_windows("down", i)]
            hi(ws[0], ffn_tail("up", FF // W - 1))
            def p_split():
                act.wait_ge(p_turned, 1)
                act.activation(pt_hi[:].rearrange("p a b -> p (a b)"), bank[X1][:], ACT.Copy).then_inc(p_hi, 1)
            for n in range(1, NB):
                pieces = residual("down", n - 1, ws[n - 1], xt_hi, g_ple)
                if n == 1:
                    pieces[8] = [p_split]
                hi(ws[n], pieces)
            before = ws[-1]

            for w in proj_windows():
                hi(w)
            for n, w in enumerate(proj_windows()):
                if n == NB // 2:
                    square("down", NB - 1, acc_read[before.par], 2 * before.block + 2)
                    split("down", NB - 1, xt_hi, g_ple)
                act.wait_ge(stage_used, w.end())
                act.activation(pp[:, 0, n * W:(n + 1) * W], acc[w.par][0][:], ACT.Copy).then_inc(acc_read[w.par], 1)

            def gate_sigmoid(n, w):
                act.wait_ge(rstd_done, NORM["down"] + 1)
                act.wait_ge(stage_used, w.end())
                reached(act, res_done, T * n)
                for t in range(T):
                    act.activation(sg_s[:, t, :], acc[w.par][t][:], ACT.Sigmoid,
                                   scale=rstd[:, NORM["down"], t:t + 1]).then_inc(acc_read[w.par], 1)

            def gate_pieces(n, w):
                return {3: [lambda: gate_sigmoid(n, w)],
                        4: [lambda: square("gate", n, res_done, T * (n + 1))],
                        6: [lambda: split("gate", n, zt_hi, g_mix2)]}

            ws = [w for i in range(NB // 2) for w in pair_windows("gate", i)]
            hi(ws[0])
            for n in range(1, NB):
                hi(ws[n], gate_pieces(n - 1, ws[n - 1]))
            before = ws[-1]

            def r_evac(b, w):
                act.wait_ge(rstd_done, NORM["gate"] + 1)
                act.wait_ge(stage_used, w.end())
                act.activation(s_s[:, w.par, 0, :], acc[w.par][0][:], ACT.Copy,
                               scale=rstd[:, NORM["gate"], 0:1]).then_inc(acc_read[w.par], 1)

            def r_copy_qt(b):
                act.wait_ge(r_turned, b + 1)
                act.activation(rqt_s[:], bank[T1][:, 0:S], ACT.Copy, scale=AD ** -0.5).then_inc(r_qt, 1)
                act.activation(rkt_s[:], bank[T1][:, S:2 * S], ACT.Copy).then_inc(bank_read[T1], 1)

            def r_softmax(b):
                act.wait_ge(r_nmax, b + 1)
                for hh in range(2):
                    act.activation(rp_s[:, hh, 0:P], bank[X1 + hh][:, 0:P], ACT.Exp, bias=A_NMX[:, 2 * hh:2 * hh + 1],
                                   accum_out=A_SUM[:, 2 * hh:2 * hh + 1]).then_inc(r_exp, 1)
                    act.activation(rp_s[:, hh, P:P + S], bank[X1 + hh][:, P:P + S], ACT.Exp,
                                   bias=A_NMX[:, 2 * hh + 1:2 * hh + 2],
                                   accum_out=A_SUM[:, 2 * hh + 1:2 * hh + 2]).then_inc(bank_read[X1 + hh], 1)

            def r_copy_pt(b):
                act.wait_ge(r_pturned, 2 * b + 1)
                act.activation(rpt_s[:, 0, :], bank[T1][:, 0:S + P], ACT.Copy).then_inc(bank_read[T1], 1)

            def r_split(b):
                act.wait_ge(r_out, b + 1)
                act.activation(xt_hi[:, ds(b, 1), :].rearrange("p o c -> p (o c)"), bank[X1][:, 0:S], ACT.Copy).then_inc(r_yhi, 1)

            def pool_split(g):
                act.wait_ge(y_pool, g + 1)
                for e in range(2):
                    act.activation(xt_hi[:, ds(2 * g + (AW // P + e), 1), :].rearrange("p o c -> p (o c)"), bank[X2][:, e * S:(e + 1) * S],
                                   ACT.Copy, scale=gains[:, ds(2 * g + (g_pool + e), 1)]).then_inc(y_phi, 1)

            def rel_pieces(b, w, last, pooled=None):
                after = {3: [lambda: r_evac(b, w)], 4: [lambda: r_copy_qt(b)], 6: [lambda: r_softmax(b)]}
                if last is not None:
                    after[1] = [lambda: r_copy_pt(last)]
                    after[4].insert(0, lambda: r_split(last))
                    if pooled is not None:
                        after[4].insert(1, lambda: pool_split(pooled))
                return after

            w0, w1 = pair_windows("rel", 0)
            hi(w0, gate_pieces(NB - 1, before))
            hi(w1, rel_pieces(0, w0, None))
            with act.Fori(1, AH // 4) as i:
                _, before = pair_windows("rel", i - 1)
                w0, w1 = pair_windows("rel", i)
                hi(w0, rel_pieces(2 * i - 1, before, 2 * i - 2))
                hi(w1, rel_pieces(2 * i, w0, 2 * i - 1, i - 1))

            def sig(n, w, dst, used):
                act.wait_ge(stage_used, w.end())
                reached(act, *used)
                for t in range(T):
                    act.activation(dst[:, t, :], acc[w.par][t][:], ACT.Sigmoid,
                                   scale=rstd[:, NORM["gate"], t:t + 1]).then_inc(acc_read[w.par], 1)

            def mix_body(n, pieces, pieces_b={}):
                ga, gb, ba, bb = mix_windows(n)
                hi(ga, pieces)
                hi(gb, {**pieces_b, 3: [lambda: sig(n, ga, sga, (merged_made, T * n))]})
                hi(ba, {3: [lambda: sig(n, gb, sgb, (merged_made, T * n))]})
                hi(bb)

            last = AH // 2 - 1
            _, before = pair_windows("rel", AH // 4 - 1)
            mix_body(0, rel_pieces(last, before, last - 1),
                     {1: [lambda: r_copy_pt(last)], 4: [lambda: r_split(last), lambda: pool_split(G - 1)]})
            with act.Fori(1, NB) as n:
                mix_body(n, {5: [lambda: split("mix", n - 1, mt_hi, None)]})

            ws = [w for i in range(NB // 2) for w in pair_windows("out2", i)]
            hi(ws[0], {5: [lambda: split("mix", NB - 1, mt_hi, None)]})
            for n in range(1, NB):
                hi(ws[n], residual("out2", n - 1, ws[n - 1], xt_hi, g_ffn2))
            before = ws[-1]

            ffn("up2", 0, residual("out2", NB - 1, before, xt_hi, g_ffn2))
            with act.Fori(1, FF // W) as i:
                ffn("up2", i, ffn_tail("up2", i - 1))
            ws = [w for i in range(NB // 2) for w in pair_windows("down2", i)]
            hi(ws[0], ffn_tail("up2", FF // W - 1))
            act.wait_ge(stage_used, ws[0].stages_to(0))
            act.dma_start(gfin[:], A["norm_final_2"].rearrange("(o c) -> o c", o=1).partition_broadcast(P).rearrange("p o c -> p (o c)")).then_inc(gfin_landed, 16)
            for n in range(1, NB):
                hi(ws[n], {3: [lambda: square("down2", n - 1, acc_read[ws[n - 1].par], 2 * ws[n - 1].block + 2)]})
            square("down2", NB - 1, acc_read[ws[-1].par], 2 * ws[-1].block + 2)

        @block.vector
        def _(dve):
            def lo(w, after={}):
                for j in range(w.n):
                    s = w.slot(j)
                    dve.wait_ge(hi_made, w.stages_to(j))
                    dve.tensor_tensor(wlo[:, s, :, 0:w.width], raw[:, s, :, 0:w.width],
                                      whi[:, s, :, 0:w.width].bitcast(F32), ALU.subtract).then_inc(lo_made, 1)
                    for piece in after.get(j, []):
                        piece()

            def flat(ap):
                return ap.rearrange("p o c -> p (o c)")

            def split(phase, n, dst_hi, dst_lo, gain):
                r = RES0[phase] + n
                for kk in range(4):
                    dve.wait_ge(split_hi, 4 * r + 2 * (kk // 2) + 2)
                    k = 4 * n + kk
                    src = bank[kk // 2][:, (kk % 2) * S:(kk % 2 + 1) * S]
                    high = flat(dst_hi[:, ds(k, 1), :]).bitcast(F32)
                    low = flat(dst_lo[:, ds(k, 1), :])
                    scale = 1.0 if gain is None else gains[:, gain + k:gain + k + 1]
                    done = dve.scalar_tensor_tensor(low, src, scale, high, ALU.mult, ALU.subtract)
                    if kk % 2:
                        done.then_inc(bank_read[kk // 2], 1)

            def add(n, w):
                dve.wait_ge(stage_used, w.end())
                for t in range(T):
                    x = xres[:, t, n * W:(n + 1) * W]
                    dve.tensor_tensor(x, acc[w.par][t][:], x, ALU.add).then_inc(acc_read[w.par], 1)

            def mean(phase):
                norm = NORM[phase]
                dve.wait_ge(square_done, T * NB * (norm + 1))
                dve.tensor_reduce(meansq[:, norm, :], sumsq[:, norm, :, :], AX.X, ALU.add).then_inc(meansq_done, 1)

            for n in range(NB):
                split("init", n, xt_hi, xt_lo, g_mix)
            mean("init")
            dve.wait_ge(gate_w_hi, 1)
            dve.tensor_tensor(wg_lo[:], wg_raw[:], wg_hi[:].bitcast(F32), ALU.subtract).then_inc(gate_w_lo, 1)

            step = [0]

            def logit(instruction):
                step[0] += 1
                instruction.then_inc(logit_step, 1)
                dve.wait_ge(logit_step, step[0])

            FG = slice(MH, NG)

            def logits():
                dve.wait_ge(logits_made, 1)
                dve.wait_ge(rstd_done, 1)
                dve.wait_ge(bias_landed, 32)
                for t in range(T):
                    done = dve.scalar_tensor_tensor(gl[:, t, :], bank[X2][:, NG * t:NG * (t + 1)], rstd[:, 0, t:t + 1],
                                                    bias_bc[:], ALU.mult, ALU.add)
                done.then_inc(bank_read[X2], 1)
                dve.wait_ge(bank_read[X2], 1)
                logit(dve.tensor_scalar(lsx[:, 0], gl[:, :, FG], -1.0, None, ALU.mult))
                logit(dve.tensor_tensor(lsx[:, 1], lsx[:, 0], gl[:, :, FG], ALU.max))

            def log_sigmoid():
                dve.wait_ge(logit_exp, 1)
                logit(dve.tensor_scalar(lsx[:, 3], lsx[:, 2], 2.0, None, ALU.add))
                logit(dve.reciprocal(lsx[:, 4], lsx[:, 3]))
                logit(dve.tensor_tensor(lsx[:, 5], lsx[:, 2], lsx[:, 4], ALU.mult))
                logit(dve.tensor_tensor(lsx[:, 6], lsx[:, 5], lsx[:, 5], ALU.mult))
                logit(dve.tensor_scalar(lsx[:, 7], lsx[:, 6], 1.0 / 17, None, ALU.mult))
                for odd in (15, 13, 11, 9, 7, 5, 3):
                    logit(dve.scalar_tensor_tensor(lsx[:, 7], lsx[:, 7], 1.0 / odd, lsx[:, 6], ALU.add, ALU.mult))
                logit(dve.scalar_tensor_tensor(lsx[:, 7], lsx[:, 7], 1.0, lsx[:, 5], ALU.add, ALU.mult))
                logit(dve.tensor_scalar(lsx[:, 3], gl[:, :, FG], 0.0, None, ALU.min))
                logit(dve.scalar_tensor_tensor(gl[:, :, FG], lsx[:, 7], -2.0, lsx[:, 3], ALU.mult, ALU.add))

            def row_scans():
                dve.wait_ge(rows_turned, 1)
                dve.wait_ge(const_made, N_CONST)
                one = ones[0:MH, :]
                dve.tensor_tensor_scan(crow[0:MH, 0], one, bank[X1][0:MH, S:2 * S], 0.0, ALU.mult, ALU.add).then_inc(row_step, 1)
                dve.tensor_tensor_scan(crow[0:FH, 4], ones[0:FH, :], bank[X2][0:FH, 0:S], 0.0, ALU.mult, ALU.add)\
                    .then_inc(bank_read[X2], 1)
                dve.wait_ge(row_step, 1)
                dve.tensor_tensor(crow[0:MH, 1], bank[X1][0:MH, 0:S], crow[0:MH, 0], ALU.subtract).then_inc(bank_read[X1], 1)
                dve.wait_ge(bank_read[X1], 2)
                dve.tensor_tensor_scan(crow[0:MH, 2], one, crow[0:MH, 1], 0.0, ALU.mult, ALU.max).then_inc(row_step, 1)
                dve.wait_ge(row_step, 2)
                dve.tensor_tensor(crow[0:MH, 3], crow[0:MH, 2], crow[0:MH, 0], ALU.add).then_inc(row_step, 1)
                dve.tensor_scalar(crow[0:FH, 5], crow[0:FH, 4], -1.0, None, ALU.mult).then_inc(row_step, 1)
                dve.wait_ge(row_step, 4)
                dve.tensor_scalar(crow[0:MH, 2], crow[0:MH, 2], -1.0, None, ALU.mult).then_inc(row_step, 1)

            def col_copy():
                dve.wait_ge(cols_turned, 1)
                dve.tensor_copy(cols[:, :, :].rearrange("p t c -> p (t c)"), bank[X1][:, 0:T * NG]).then_inc(bank_read[X1], 1)

            def m_evac_qk(w):
                dve.wait_ge(stage_used, w.end())
                dve.tensor_scalar(qk_s[:, 1, :], acc[0][1][:], rstd[:, 0, 1:2], None, ALU.mult).then_inc(acc_read[0], 1)

            def m_copy_kt(h):
                dve.wait_ge(m_turned, 2 * h + 2)
                dve.tensor_scalar(kt_s[:, :, :].rearrange("p a b -> p (a b)"), bank[T2][:], MD ** -0.5, None, ALU.mult)\
                    .then_inc(bank_read[T2], 1)

            def m_log_decay(h):
                dve.wait_ge(m_scored, 2 * h + 1)
                dve.tensor_tensor(dw_s[:], bank[X2][:, 0:S + P], mask_m[:], ALU.add).then_inc(bank_read[X2], 1)

            def m_weights(h):
                dve.wait_ge(m_scored, 2 * h + 2)
                dve.wait_ge(m_weight, 2 * h + 2)
                dve.tensor_tensor(pt_s[:], bank[X1][:, 0:S + P], dw_s[:], ALU.mult).then_inc(bank_read[X1], 1)

            def m_evac_v(h, w):
                dve.wait_ge(stage_used, w.end())
                for t in range(T):
                    dve.wait_ge(m_so, T * h + t + 1)
                    dve.tensor_scalar(v_s[:, t, :], acc[1][t][:, 0:MD], rstd[:, 0, t:t + 1], None, ALU.mult)\
                        .then_inc(acc_read[1], 1)

            def m_denominator(h):
                dve.wait_ge(m_den, h + 1)
                dve.tensor_scalar(M_ND, bank[T2][:, 0:T], -1.0, None, ALU.mult).then_inc(m_nd, 1)
                dve.wait_ge(m_nd, 3 * h + 1)
                dve.tensor_tensor(M_DEN, bank[T2][:, 0:T], M_ND, ALU.max).then_inc(bank_read[T2], 1)
                dve.wait_ge(bank_read[T2], USE0[T2]["mlstm"] + 3 * h + 2)
                dve.tensor_tensor(M_DEN, M_DEN, em[:, :, ds(h, 1)].rearrange("p t o -> p (t o)"), ALU.max).then_inc(m_nd, 1)
                dve.wait_ge(m_nd, 3 * h + 2)
                dve.reciprocal(M_RDEN, M_DEN).then_inc(m_rden, 1)

            def m_mean(h):
                dve.wait_ge(m_sq, T * h + T)
                dve.tensor_scalar(M_MS, M_MS, 1.0 / MD, EPS, ALU.mult, ALU.add).then_inc(m_eps, 1)

            def m_output(h):
                dve.wait_ge(m_rs, h + 1)
                dve.tensor_tensor(M_COMB, M_RDEN, M_RS, ALU.mult).then_inc(m_nd, 1)
                dve.wait_ge(m_nd, 3 * h + 3)
                for t in range(T):
                    done = dve.scalar_tensor_tensor(y_s[:, t, :], bank[T1][:, t * MD:(t + 1) * MD], M_COMB[:, t:t + 1],
                                                    so_s[:, t, :], ALU.mult, ALU.mult)
                done.then_inc(bank_read[T1], 1)

            def m_split(h):
                dve.wait_ge(m_yhi, 2 * h + 2)
                for d in range(2):
                    done = dve.scalar_tensor_tensor(
                        flat(yt_lo[:, ds(2 * h + d, 1), :]), bank[T2][:, d * S:(d + 1) * S],
                        gains[:, ds(2 * h + (g_mlstm + d), 1)],
                        flat(yt_hi[:, ds(2 * h + d, 1), :]).bitcast(F32), ALU.mult, ALU.subtract)
                done.then_inc(bank_read[T2], 1)

            def mlstm(h, first):
                a, b = pair_windows("mlstm", h)
                after_b = {3: [lambda: m_evac_qk(a)], 4: [lambda: m_copy_kt(h)],
                           6: [lambda: m_log_decay(h)], 7: [lambda: m_weights(h)]}
                if first:
                    after_a = {1: [logits], 2: [log_sigmoid], 4: [row_scans], 6: [col_copy]}
                else:
                    prev = h - 1
                    pa, pb = pair_windows("mlstm", prev)
                    after_a = {3: [lambda: m_evac_v(prev, pb)], 5: [lambda: m_denominator(prev)],
                               7: [lambda: m_mean(prev), lambda: m_output(prev)]}
                    after_b[1] = [lambda: m_split(prev)]
                lo(a, after_a)
                lo(b, after_b)

            mlstm(0, True)
            with dve.Fori(1, MH) as h:
                mlstm(h, False)

            def f_evac(b, w):
                dve.wait_ge(stage_used, w.end())
                dve.tensor_scalar(f_s[:, w.par, 1, :], acc[w.par][1][:, 0:3 * FD], rstd[:, 0, 1:2], None, ALU.mult)\
                    .then_inc(acc_read[w.par], 1)

            def f_sums(b):
                dve.wait_ge(f_sq, b + 1)
                dve.tensor_reduce(F_SS, fsq_s[:].rearrange("p t (j d) -> p (t j) d", d=FD), AX.X, ALU.add).then_inc(f_ss, 1)
                dve.wait_ge(f_ss, b + 1)
                dve.tensor_scalar(F_SS, F_SS, 1.0 / FD, EPS, ALU.mult, ALU.add).then_inc(f_eps, 1)

            def f_row_bias(b):
                dve.wait_ge(f_scored, 2 * b + 1)
                dve.scalar_tensor_tensor(fg_s[:, 0:P], bank[X2][:, 0:P], cols[:, 0, ds(b + 2 * MH, 1)], mask_f[:, 0:P],
                                         ALU.add, ALU.add)
                dve.scalar_tensor_tensor(fg_s[:, P:P + S], bank[X2][:, 0:S], cols[:, 1, ds(b + 2 * MH, 1)], mask_f[:, P:P + S],
                                         ALU.add, ALU.add).then_inc(bank_read[X2], 1)

            def f_logits(b):
                dve.wait_ge(f_scored, 2 * b + 2)
                dve.wait_ge(bank_read[X2], USE0[X2]["fox"] + 2 * b + 1)
                dve.scalar_tensor_tensor(fg_s[:], bank[X1][:, 0:S + P], FD ** -0.5, fg_s[:], ALU.mult, ALU.add)\
                    .then_inc(bank_read[X1], 1)
                dve.wait_ge(bank_read[X1], USE0[X1]["fox"] + b + 1)
                dve.tensor_reduce(F_MX[:, 0:1], fg_s[:, 0:P], AX.X, ALU.max)
                dve.tensor_reduce(F_MX[:, 1:2], fg_s[:, P:P + S], AX.X, ALU.max).then_inc(f_max, 1)
                dve.wait_ge(f_max, b + 1)
                dve.tensor_scalar(F_NMX, F_MX, -1.0, None, ALU.mult).then_inc(f_nmax, 1)

            def f_normalise(b):
                dve.wait_ge(f_exp, 2 * b + 2)
                dve.reciprocal(F_RINV, F_SUM).then_inc(f_rinv, 1)
                dve.wait_ge(f_rinv, b + 1)
                dve.tensor_scalar(fp_s[:, 0:P], fp_s[:, 0:P], F_RINV[:, 0:1], None, ALU.mult)
                dve.tensor_scalar(fp_s[:, P:P + S], fp_s[:, P:P + S], F_RINV[:, 1:2], None, ALU.mult).then_inc(f_probs, 1)

            def f_split(b):
                dve.wait_ge(f_yhi, b + 1)
                dve.tensor_tensor(flat(yt_lo[:, ds(b + MW // P, 1), :]), bank[X2][:, 0:S],
                                  flat(yt_hi[:, ds(b + MW // P, 1), :]).bitcast(F32), ALU.subtract).then_inc(bank_read[X2], 1)

            def fox_pieces(b, w, last=None):
                after = {3: [lambda: f_evac(b, w)], 4: [lambda: f_sums(b)],
                         6: [lambda: f_row_bias(b)], 7: [lambda: f_logits(b)]}
                if last is not None:
                    after[0] = [lambda: f_normalise(last)]
                    after[5] = [lambda: f_split(last)]
                return after

            _, m_last = pair_windows("mlstm", MH - 1)
            w0, w1 = fox_w(0)
            lo(w0, {3: [lambda: m_evac_v(MH - 1, m_last)], 5: [lambda: m_denominator(MH - 1)],
                    7: [lambda: m_mean(MH - 1), lambda: m_output(MH - 1)]})
            pieces = fox_pieces(0, w0)
            pieces[1] = [lambda: m_split(MH - 1)]
            lo(w1, pieces)
            with dve.Fori(1, FH // 2) as i:
                _, before = fox_w(i - 1)
                w0, w1 = fox_w(i)
                lo(w0, fox_pieces(2 * i - 1, before, 2 * i - 2))
                lo(w1, fox_pieces(2 * i, w0, 2 * i - 1))

            def residual(phase, n, w, dst_hi, dst_lo, gain, final=False):
                after = {3: [lambda: add(n, w)], 5: [lambda: split(phase, n, dst_hi, dst_lo, gain)]}
                if final:
                    after[4] = [lambda: mean(phase)]
                return after

            ws = [w for i in range(NB // 2) for w in pair_windows("out", i)]
            _, before = fox_w(FH // 2 - 1)
            lo(ws[0], {0: [lambda: f_normalise(FH - 2)], 3: [lambda: f_evac(FH - 1, before), lambda: f_sums(FH - 1)],
                       4: [lambda: f_split(FH - 2), lambda: f_row_bias(FH - 1), lambda: f_logits(FH - 1)],
                       5: [lambda: f_normalise(FH - 1)], 7: [lambda: f_split(FH - 1)]})
            for n in range(1, NB):
                lo(ws[n], residual("out", n - 1, ws[n - 1], xt_hi, xt_lo, g_ffn))
            before = ws[-1]

            def ffn_evac(phase, i, w):
                f, norm = FFN0[phase] + i, NORM["out" if phase == "up" else "out2"]
                dve.wait_ge(stage_used, w.end())
                for t in range(T):
                    dve.tensor_scalar(g_s[:, t, :], acc[1][t][:], rstd[:, norm, t:t + 1], None, ALU.mult)\
                        .then_inc(acc_read[1], 1)

            def conv(i, tap):
                f = FFN0["up"] + i
                if tap == 2:
                    reached(dve, hid_hi, f)
                else:
                    dve.wait_ge(conv_step, 2 * i + 2 - tap)
                for kk in range(4):
                    half_ = kk // 2
                    dve.wait_ge(a_turned, 2 * f + 1 + half_)
                    src = bank[half_][:, (kk % 2) * S:(kk % 2 + 1) * S]
                    k = 4 * i + kk
                    taps = convs[:, ds(k + KF * tap, 1)]
                    if tap == 2:
                        done = dve.tensor_scalar(hid[:, kk, :], src, taps, convs[:, ds(k + KF * 3, 1)], ALU.mult, ALU.add)
                    else:
                        shift = 2 - tap
                        done = dve.scalar_tensor_tensor(hid[:, kk, shift:S], src[:, 0:S - shift], taps, hid[:, kk, shift:S],
                                                        ALU.mult, ALU.add)
                    if tap == 0 and kk % 2:
                        done.then_inc(bank_read[half_], 1)
                    elif kk == 3:
                        done.then_inc(conv_step, 1)

            def ffn_product(phase, i):
                f = FFN0[phase] + i
                if phase == "up":
                    dve.wait_ge(hid_act, i + 1)
                else:
                    dve.wait_ge(bank_read[T2], USE0[T2][phase] + i + 1)
                for half_ in range(2):
                    dve.wait_ge(g_turned, 2 * f + 1 + half_)
                    hh = hid[:, 2 * half_:2 * half_ + 2, :].rearrange("p a b -> p (a b)")
                    dve.tensor_tensor(hh, bank[X1 + half_][:], hh, ALU.mult).then_inc(bank_read[X1 + half_], 1)

            def ffn_split(phase, i):
                dve.wait_ge(hid_hi, FFN0[phase] + i + 1)
                dve.tensor_tensor(ht_lo[:, ds(4 * i, 4), :], hid[:], ht_hi[:, ds(4 * i, 4), :].bitcast(F32), ALU.subtract)\
                    .then_inc(hid_lo, 1)

            def ffn_tail(phase, i):
                w = pair_windows(phase, i)[1]
                return {3: [lambda: ffn_evac(phase, i, w)], 5: [lambda: ffn_product(phase, i)],
                        6: [lambda: ffn_split(phase, i)]}

            def ffn(phase, i, pieces):
                a, g = pair_windows(phase, i)
                lo(a, pieces)
                lo(g, {5: [lambda: conv(i, 2)], 6: [lambda: conv(i, 1)], 7: [lambda: conv(i, 0)]} if phase == "up" else {})

            ffn("up", 0, residual("out", NB - 1, before, xt_hi, xt_lo, g_ffn, True))
            with dve.Fori(1, FF // W) as i:
                ffn("up", i, ffn_tail("up", i - 1))
            ws = [w for i in range(NB // 2) for w in pair_windows("down", i)]
            lo(ws[0], ffn_tail("up", FF // W - 1))
            def p_split():
                dve.wait_ge(p_hi, 1)
                dve.tensor_tensor(pt_lo[:].rearrange("p a b -> p (a b)"), bank[X1][:],
                                  pt_hi[:].rearrange("p a b -> p (a b)").bitcast(F32), ALU.subtract).then_inc(bank_read[X1], 1)
            for n in range(1, NB):
                pieces = residual("down", n - 1, ws[n - 1], xt_hi, xt_lo, g_ple)
                if n == 1:
                    pieces[8] = [p_split]
                lo(ws[n], pieces)
            before = ws[-1]

            for w in proj_windows():
                lo(w)
            add(NB - 1, before)
            for n, w in enumerate(proj_windows()):
                if n == NB // 2:
                    mean("down")
                    split("down", NB - 1, xt_hi, xt_lo, g_ple)
                dve.wait_ge(stage_used, w.end())
                dve.tensor_copy(pp[:, 1, n * W:(n + 1) * W], acc[w.par][1][:]).then_inc(acc_read[w.par], 1)

            def gate_add(n, w):
                dve.wait_ge(acc_read[w.par], 2 * w.block + 2)
                dve.wait_ge(acc_read[n % 2], 2 * proj_windows()[n].block + 2)
                for t in range(T):
                    dve.tensor_tensor(sg_s[:, t, :], sg_s[:, t, :], pp[:, t, n * W:(n + 1) * W], ALU.mult).then_inc(gated, 1)
                for t in range(T):
                    dve.wait_ge(gated, T * n + t + 1)
                    x = xres[:, t, n * W:(n + 1) * W]
                    dve.tensor_tensor(x, x, sg_s[:, t, :], ALU.add).then_inc(res_done, 1)

            def gate_pieces(n, w, final=False):
                after = {3: [lambda: gate_add(n, w)], 6: [lambda: split("gate", n, zt_hi, zt_lo, g_mix2)]}
                if final:
                    after[5] = [lambda: mean("gate")]
                return after

            ws = [w for i in range(NB // 2) for w in pair_windows("gate", i)]
            lo(ws[0])
            for n in range(1, NB):
                lo(ws[n], gate_pieces(n - 1, ws[n - 1]))
            before = ws[-1]

            def r_evac(b, w):
                dve.wait_ge(rstd_done, NORM["gate"] + 1)
                dve.wait_ge(stage_used, w.end())
                dve.tensor_scalar(s_s[:, w.par, 1, :], acc[w.par][1][:], rstd[:, NORM["gate"], 1:2], None, ALU.mult)\
                    .then_inc(acc_read[w.par], 1)

            def r_pool(b, par):
                dve.wait_ge(r_pooled, b + 1)
                dve.tensor_copy(dt_s[:, par, :], bank[T2][:, 0:S]).then_inc(bank_read[T2], 1)

            def r_maxima(b):
                for hh in range(2):
                    dve.wait_ge(r_scored, 2 * b + hh + 1)
                    dve.tensor_reduce(A_MX[:, 2 * hh:2 * hh + 1], bank[X1 + hh][:, 0:P], AX.X, ALU.max)
                    done = dve.tensor_reduce(A_MX[:, 2 * hh + 1:2 * hh + 2], bank[X1 + hh][:, P:P + S], AX.X, ALU.max)
                done.then_inc(r_max, 1)
                dve.wait_ge(r_max, b + 1)
                dve.tensor_scalar(A_NMX, A_MX, -1.0, None, ALU.mult).then_inc(r_nmax, 1)

            def r_normalise(b, use):
                dve.wait_ge(bank_read[X2], USE0[X2]["rel"] + use + 1)
                dve.reciprocal(A_RINV, A_SUM).then_inc(r_rinv, 1)
                dve.wait_ge(r_rinv, b + 1)
                for hh in range(2):
                    dve.tensor_scalar(rp_s[:, hh, 0:P], rp_s[:, hh, 0:P], A_RINV[:, 2 * hh:2 * hh + 1], None, ALU.mult)
                    done = dve.tensor_scalar(rp_s[:, hh, P:P + S], rp_s[:, hh, P:P + S], A_RINV[:, 2 * hh + 1:2 * hh + 2],
                                             None, ALU.mult)
                done.then_inc(r_probs, 1)

            def r_copy_pt(b):
                dve.wait_ge(r_pturned, 2 * b + 2)
                dve.tensor_copy(rpt_s[:, 1, :], bank[T2][:, 0:S + P]).then_inc(bank_read[T2], 1)

            def r_split(b):
                dve.wait_ge(r_yhi, b + 1)
                dve.tensor_tensor(flat(xt_lo[:, ds(b, 1), :]), bank[X1][:, 0:S],
                                  flat(xt_hi[:, ds(b, 1), :]).bitcast(F32), ALU.subtract).then_inc(bank_read[X1], 1)

            def pool_split(g):
                dve.wait_ge(y_phi, 2 * g + 2)
                for e in range(2):
                    k = 2 * g + (AW // P + e)
                    done = dve.scalar_tensor_tensor(flat(xt_lo[:, ds(k, 1), :]), bank[X2][:, e * S:(e + 1) * S],
                                                    gains[:, ds(2 * g + (g_pool + e), 1)],
                                                    flat(xt_hi[:, ds(k, 1), :]).bitcast(F32), ALU.mult, ALU.subtract)
                done.then_inc(bank_read[X2], 1)

            def rel_pieces(b, w, last, use, pooled=None):
                after = {3: [lambda: r_evac(b, w)], 4: [lambda: r_pool(b, w.par)], 5: [lambda: r_maxima(b)],
                         7: [lambda: r_normalise(b, use)]}
                if last is not None:
                    after[1] = [lambda: r_copy_pt(last)]
                    after[4].insert(0, lambda: r_split(last))
                    if pooled is not None:
                        after[4].insert(1, lambda: pool_split(pooled))
                return after

            w0, w1 = pair_windows("rel", 0)
            lo(w0, gate_pieces(NB - 1, before, True))
            lo(w1, rel_pieces(0, w0, None, 0))
            with dve.Fori(1, AH // 4) as i:
                _, before = pair_windows("rel", i - 1)
                w0, w1 = pair_windows("rel", i)
                lo(w0, rel_pieces(2 * i - 1, before, 2 * i - 2, 3 * i - 2))
                lo(w1, rel_pieces(2 * i, w0, 2 * i - 1, 3 * i, i - 1))

            def mix_a(n, w, ga):
                dve.wait_ge(acc_read[0], 2 * ga.block + 2)
                dve.wait_ge(stage_used, w.end())
                for t in range(T):
                    dve.tensor_tensor(merged[:, t, :], acc[0][t][:], sga[:, t, :], ALU.mult).then_inc(acc_read[0], 1)

            def mix_b(n, w, gb):
                dve.wait_ge(acc_read[1], 2 * gb.block + 2)
                dve.wait_ge(stage_used, w.end())
                for t in range(T):
                    dve.tensor_tensor(sgb[:, t, :], acc[1][t][:], sgb[:, t, :], ALU.mult).then_inc(acc_read[1], 1)
                dve.wait_ge(acc_read[0], 2 * w.block + 2)
                for t in range(T):
                    dve.wait_ge(acc_read[1], 2 * w.block + t + 1)
                    dve.tensor_tensor(merged[:, t, :], merged[:, t, :], sgb[:, t, :], ALU.add).then_inc(merged_made, 1)

            def mix_body(n, pieces, pieces_b={}):
                ga, gb, ba, bb = mix_windows(n)
                lo(ga, pieces)
                lo(gb, pieces_b)
                lo(ba)
                lo(bb, {3: [lambda: mix_a(n, ba, ga)]})

            def mix_tail(n):
                ga, gb, ba, bb = mix_windows(n)
                return {3: [lambda: mix_b(n, bb, gb)], 5: [lambda: split("mix", n, mt_hi, mt_lo, None)]}

            last = AH // 2 - 1
            _, before = pair_windows("rel", AH // 4 - 1)
            mix_body(0, rel_pieces(last, before, last - 1, 3 * (AH // 4) - 2),
                     {1: [lambda: r_copy_pt(last)], 4: [lambda: r_split(last), lambda: pool_split(G - 1)]})
            with dve.Fori(1, NB) as n:
                mix_body(n, mix_tail(n - 1))

            ws = [w for i in range(NB // 2) for w in pair_windows("out2", i)]
            lo(ws[0], mix_tail(NB - 1))
            for n in range(1, NB):
                lo(ws[n], residual("out2", n - 1, ws[n - 1], xt_hi, xt_lo, g_ffn2))
            before = ws[-1]
            ffn("up2", 0, residual("out2", NB - 1, before, xt_hi, xt_lo, g_ffn2, True))
            with dve.Fori(1, FF // W) as i:
                ffn("up2", i, ffn_tail("up2", i - 1))
            ws = [w for i in range(NB // 2) for w in pair_windows("down2", i)]
            lo(ws[0], ffn_tail("up2", FF // W - 1))
            for n in range(1, NB):
                lo(ws[n], {3: [lambda: add(n - 1, ws[n - 1])]})
            add(NB - 1, ws[-1])
            mean("down2")
            dve.wait_ge(rstd_done, NORM["down2"] + 1)
            dve.wait_ge(gfin_landed, 16)
            for n in range(NB):
                for t in range(T):
                    x = xres[:, t, n * W:(n + 1) * W]
                    dve.scalar_tensor_tensor(x, x, rstd[:, NORM["down2"], t:t + 1], gfin[:, n * W:(n + 1) * W],
                                             ALU.mult, ALU.mult).then_inc(out_made, 1)

        @block.tensor
        def _(pe):
            def free(b, phase, n):
                reached(pe, bank_read[b], USE0[b][phase] + n)

            def multiply(w, high, low, k0=0, before={}, after={}):
                reached(pe, acc_read[w.par], 2 * w.block)
                for j in range(w.n):
                    for piece in before.get(j, []):
                        piece()
                    s = w.slot(j)
                    pe.wait_ge(lo_made, w.stages_to(j))
                    for kk in range(KS):
                        k = k0 + KS * j + kk
                        for t in range(T):
                            out_ = acc[w.par][t][:, 0:w.width]
                            h_, l_ = high[:, k, t * P:(t + 1) * P], low[:, k, t * P:(t + 1) * P]
                            wh_, wl_ = whi[:, s, kk, 0:w.width], wlo[:, s, kk, 0:w.width]
                            pe.matmul(out_, h_, wh_, start=(j == 0 and kk == 0), stop=False)
                            pe.matmul(out_, h_, wl_, start=False, stop=False)
                            done = pe.matmul(out_, l_, wh_, start=False, stop=(j == w.n - 1 and kk == KS - 1))
                    done.then_inc(stage_used, 1)
                    for piece in after.get(j, []):
                        piece()

            def turn(src, phase, n, ready, count):
                if ready is not None:
                    pe.wait_ge(ready, count)
                for half_ in range(2):
                    free(half_, phase, n)
                    for kk in range(2):
                        for t in range(T):
                            c = (2 * half_ + kk) * P
                            done = pe.transpose(bank[half_][:, kk * S + t * P:kk * S + (t + 1) * P], src(t, c), ident[:])
                    done.then_inc(res_turned, 1)

            def split_ready(phase, n):
                return lambda: pe.wait_ge(bank_read[T2], USE0[T2][phase] + n + 1)

            def of_x(n):
                return lambda t, c: xres[:, t, n * W + c:n * W + c + P]

            pe.wait_ge(const_made, N_CONST)
            pe.wait_ge(gains_landed, 16 * 9)
            pe.transpose(bank[X1][:, 0:NGAIN], gain_rows[0:NGAIN, :], ident[0:NGAIN, 0:NGAIN])
            pe.wait_ge(convs_landed, 16 * 4)
            for r in range(2):
                done = pe.transpose(bank[X1][:, P + r * 2 * KF:P + (r + 1) * 2 * KF], conv_rows[:, r, :],
                                    ident[0:2 * KF, 0:2 * KF])
            done.then_inc(gains_turned, 1)
            for n in range(NB):
                turn(of_x(n), "init", n, x_landed[n], 16)
            split_ready("init", NB - 1)()

            pe.wait_ge(gate_w_lo, 1)
            for t in range(T):
                for k in range(KD):
                    h_, l_ = xt_hi[:, k, t * P:(t + 1) * P], xt_lo[:, k, t * P:(t + 1) * P]
                    out_ = bank[X2][:, t * NG:(t + 1) * NG]
                    pe.matmul(out_, h_, wg_hi[:, k, :], start=(k == 0), stop=False)
                    pe.matmul(out_, h_, wg_lo[:, k, :], start=False, stop=False)
                    done = pe.matmul(out_, l_, wg_hi[:, k, :], start=False, stop=(k == KD - 1))
            done.then_inc(logits_made, 1)

            def rows_turn():
                pe.wait_ge(logit_step, N_LOGIT)
                free(X1, "init", 1)
                free(X2, "init", 1)
                for t in range(T):
                    pe.transpose(bank[X1][0:MH, t * P:(t + 1) * P], gl[:, t, 0:MH], ident[:])
                    pe.transpose(bank[X1][0:MH, S + t * P:S + (t + 1) * P], gl[:, t, MH:2 * MH], ident[:])
                    done = pe.transpose(bank[X2][0:FH, t * P:(t + 1) * P], gl[:, t, 2 * MH:NG], ident[:])
                done.then_inc(rows_turned, 1)

            def cols_turn():
                pe.wait_ge(row_step, 5)
                free(X1, "init", 2)
                for t in range(T):
                    tok = slice(t * P, (t + 1) * P)
                    for row, n, c in ((1, MH, 0), (3, MH, MH), (4, FH, 2 * MH)):
                        done = pe.transpose(bank[X1][:, t * NG + c:t * NG + c + n], crow[0:n, row, tok], ident[0:n, 0:n])
                done.then_inc(cols_turned, 1)

            def m_turn(h, w):
                pe.wait_ge(acc_read[0], 2 * w.block + 2)
                for j in range(2):
                    free(T1 + j, "mlstm", (2 + j) * h)
                    for d in range(2):
                        for t in range(T):
                            c = j * MD + d * P
                            done = pe.transpose(bank[T1 + j][:, d * S + t * P:d * S + (t + 1) * P], qk_s[:, t, c:c + P], ident[:])
                    done.then_inc(m_turned, 1)

            def m_scores(h):
                free(X2, "mlstm", h)
                if isinstance(h, int):
                    pe.wait_ge(diag_made, 2)
                row = diag_m[:, ds(h, 1), :].rearrange("p o c -> p (o c)")
                row1 = diag_m[:, ds(h, 1), P:S].rearrange("p o c -> p (o c)")
                pe.matmul(bank[X2][:, 0:S], ones[0:MH, 0:P], row, start=True, stop=True)
                pe.matmul(bank[X2][:, S:S + P], ones[0:MH, 0:P], row1, start=True, stop=True).then_inc(m_scored, 1)
                pe.wait_ge(bank_read[T1], USE0[T1]["mlstm"] + 2 * h + 1)
                pe.wait_ge(bank_read[T2], USE0[T2]["mlstm"] + 3 * h + 1)
                free(X1, "mlstm", h)
                for s, c0 in ((0, 0), (1, S)):
                    for d in range(2):
                        done = pe.matmul(bank[X1][:, c0:c0 + S - s * P], kt_s[:, d, s * P:(s + 1) * P], qt_s[:, d, s * P:S],
                                         start=(d == 0), stop=(d == 1))
                done.then_inc(m_scored, 1)

            def m_numerator(h):
                pe.wait_ge(bank_read[X1], USE0[X1]["mlstm"] + h + 1)
                pe.wait_ge(acc_read[1], 2 * (PAIR0["mlstm"] + h) + 2)
                free(T1, "mlstm", 2 * h + 1)
                free(T2, "mlstm", 3 * h + 1)
                for t in range(T):
                    for s in range(t + 1):
                        weights = pt_s[:, S:S + P] if s else pt_s[:, t * P:(t + 1) * P]
                        pe.matmul(bank[T1][:, t * MD:(t + 1) * MD], weights, v_s[:, s, :], start=(s == 0), stop=(s == t))
                        done = pe.matmul(bank[T2][:, t:t + 1], weights, ones[:, 0:1], start=(s == 0), stop=(s == t))
                done.then_inc(m_den, 1)

            def m_out_turn(h):
                pe.wait_ge(bank_read[T1], USE0[T1]["mlstm"] + 2 * h + 2)
                free(T2, "mlstm", 3 * h + 2)
                for d in range(2):
                    for t in range(T):
                        done = pe.transpose(bank[T2][:, d * S + t * P:d * S + (t + 1) * P], y_s[:, t, d * P:(d + 1) * P], ident[:])
                done.then_inc(m_yturned, 1)

            def mlstm(h, first):
                a, b = pair_windows("mlstm", h)
                after_b = {1: [lambda: m_turn(h, a)], 3: [lambda: m_scores(h)]}
                if first:
                    after_a = {2: [rows_turn], 4: [cols_turn]}
                else:
                    prev = h - 1
                    after_a = {2: [lambda: m_numerator(prev)]}
                    after_b[0] = [lambda: m_out_turn(prev)]
                multiply(a, xt_hi, xt_lo, after=after_a)
                multiply(b, xt_hi, xt_lo, after=after_b)

            mlstm(0, True)
            with pe.Fori(1, MH) as h:
                mlstm(h, False)

            def f_turn(b):
                pe.wait_ge(f_norm, b + 1)
                free(T1, "fox", b)
                for j in range(2):
                    for t in range(T):
                        done = pe.transpose(bank[T1][:, j * S + t * P:j * S + (t + 1) * P], fqk_s[:, t, j * FD:(j + 1) * FD], ident[:])
                done.then_inc(f_turned, 1)
                free(X2, "fox", 2 * b)
                pe.matmul(bank[X2][:, 0:S], ones[0:FH, 0:P], diag_f[:, ds(b, 1), :].rearrange("p o c -> p (o c)"),
                          start=True, stop=True).then_inc(f_scored, 1)

            def f_scores(b):
                pe.wait_ge(bank_read[T1], USE0[T1]["fox"] + b + 1)
                free(X1, "fox", b)
                pe.matmul(bank[X1][:, 0:P], fqt_s[:, 0:P], fkt_s[:, 0:P], start=True, stop=True)
                pe.matmul(bank[X1][:, P:P + S], fqt_s[:, P:S], fkt_s[:], start=True, stop=True).then_inc(f_scored, 1)

            def f_weights_turn(b):
                pe.wait_ge(f_probs, b + 1)
                free(T2, "fox", b)
                for n in range(3):
                    done = pe.transpose(bank[T2][:, n * P:(n + 1) * P], fp_s[:, n * P:(n + 1) * P], ident[:])
                done.then_inc(f_pturned, 1)

            def f_output(b, par):
                pe.wait_ge(bank_read[T2], USE0[T2]["fox"] + b + 1)
                free(X2, "fox", 2 * b + 1)
                pe.matmul(bank[X2][:, 0:S], f_s[:, par, 0, 2 * FD:3 * FD], fpt_s[:, 0:S], start=True, stop=False)
                pe.matmul(bank[X2][:, P:S], f_s[:, par, 1, 2 * FD:3 * FD], fpt_s[:, S:S + P], start=False, stop=True)\
                    .then_inc(f_out, 1)

            def fox_pieces(b, par, last=None):
                after = {2: [lambda: f_turn(b)], 4: [lambda: f_scores(b)], 7: [lambda: f_weights_turn(b)]}
                if last is not None:
                    after[1] = [lambda: f_output(last, 1 - par)]
                return after

            w0, w1 = fox_w(0)
            multiply(w0, xt_hi, xt_lo, after={2: [lambda: m_numerator(MH - 1)]})
            pieces = fox_pieces(0, 0)
            pieces[0] = [lambda: m_out_turn(MH - 1)]
            multiply(w1, xt_hi, xt_lo, after=pieces)
            with pe.Fori(1, FH // 2) as i:
                w0, w1 = fox_w(i)
                multiply(w0, xt_hi, xt_lo, after=fox_pieces(2 * i - 1, 1, 2 * i - 2))
                multiply(w1, xt_hi, xt_lo, after=fox_pieces(2 * i, 0, 2 * i - 1))

            def residual(phase, n, w):
                return {1: [lambda: turn(of_x(n), phase, n, acc_read[w.par], 2 * w.block + 2)]}

            ws = [w for i in range(NB // 2) for w in pair_windows("out", i)]
            multiply(ws[0], yt_hi, yt_lo,
                     before={6: [lambda: pe.wait_ge(bank_read[X2], USE0[X2]["fox"] + 2 * FH - 2)],
                             7: [lambda: pe.wait_ge(bank_read[X2], USE0[X2]["fox"] + 2 * FH)]},
                     after={1: [lambda: f_output(FH - 2, 0), lambda: f_turn(FH - 1)], 3: [lambda: f_scores(FH - 1)],
                            5: [lambda: f_weights_turn(FH - 1)], 6: [lambda: f_output(FH - 1, 1)]})
            for n in range(1, NB):
                multiply(ws[n], yt_hi, yt_lo, after=residual("out", n - 1, ws[n - 1]))

            def a_turn(phase, i, w):
                pe.wait_ge(acc_read[0], 2 * w.block + 2)
                for half_ in range(2):
                    free(half_, phase, i)
                    for kk in range(2):
                        for t in range(T):
                            c = (2 * half_ + kk) * P
                            done = pe.transpose(bank[half_][:, kk * S + t * P:kk * S + (t + 1) * P], a_s[:, t, c:c + P], ident[:])
                    done.then_inc(a_turned, 1)

            def g_turn(phase, i):
                pe.wait_ge(acc_read[1], 2 * (PAIR0[phase] + i) + 2)
                for half_ in range(2):
                    free(X1 + half_, phase, i)
                    for kk in range(2):
                        for t in range(T):
                            c = (2 * half_ + kk) * P
                            done = pe.transpose(bank[X1 + half_][:, kk * S + t * P:kk * S + (t + 1) * P], g_s[:, t, c:c + P], ident[:])
                    done.then_inc(g_turned, 1)

            def ffn(phase, i, before, after):
                a, g = pair_windows(phase, i)
                multiply(a, xt_hi, xt_lo, before=before, after=after)
                multiply(g, xt_hi, xt_lo, after={1: [lambda: a_turn(phase, i, a)]})

            def hidden_then_down(up, down, turned, w_last, extra={}):
                ffn(up, 0, {6: [split_ready(turned, NB - 1)]}, residual(turned, NB - 1, w_last))
                with pe.Fori(1, FF // W) as i:
                    ffn(up, i, {}, {1: [lambda: g_turn(up, i - 1)]})
                ws = [w for i in range(NB // 2) for w in pair_windows(down, i)]
                multiply(ws[0], ht_hi, ht_lo, after={1: [lambda: g_turn(up, FF // W - 1)]},
                         before={KF // KS - 2: [lambda: pe.wait_ge(hid_lo, FFN0[up] + FF // W)]})
                for n in range(1, NB):
                    after = {} if down == "down2" else residual(down, n - 1, ws[n - 1])
                    if n == 1:
                        after = {**after, **extra}
                    multiply(ws[n], ht_hi, ht_lo, after=after)
                return ws[-1]

            def p_turn():
                pe.wait_ge(p_landed, 16)
                free(X1, "down", 0)
                for kk in range(KS):
                    for t in range(T):
                        done = pe.transpose(bank[X1][:, kk * S + t * P:kk * S + (t + 1) * P], p_s[:, t, kk * P:(kk + 1) * P], ident[:])
                done.then_inc(p_turned, 1)

            w_last = hidden_then_down("up", "down", "out", ws[-1], {5: [p_turn]})

            pe.wait_ge(bank_read[X1], USE0[X1]["down"] + 1)
            for n, w in enumerate(proj_windows()):
                if n == NB // 2:
                    turn(of_x(NB - 1), "down", NB - 1, acc_read[w_last.par], 2 * w_last.block + 2)
                multiply(w, pt_hi, pt_lo)
            ws = [w for i in range(NB // 2) for w in pair_windows("gate", i)]

            def gate_residual(n):
                return {2: [lambda: turn(of_x(n), "gate", n, res_done, T * (n + 1))]}

            multiply(ws[0], xt_hi, xt_lo, before={6: [split_ready("down", NB - 1)]})
            for n in range(1, NB):
                multiply(ws[n], xt_hi, xt_lo, after=gate_residual(n - 1))

            def r_turn(b, w, g):
                pe.wait_ge(acc_read[w.par], 2 * w.block + 2)
                free(T1, "rel", 2 * b)
                for j in range(2):
                    for t in range(T):
                        done = pe.transpose(bank[T1][:, j * S + t * P:j * S + (t + 1) * P],
                                            s_s[:, w.par, t, j * P:(j + 1) * P], ident[:])
                done.then_inc(r_turned, 1)
                free(T2, "rel", 2 * b)
                weights = band[:, ds(g, 1), 0:S].rearrange("p o c -> p (o c)")
                weights1 = band[:, ds(g, 1), S:S + P].rearrange("p o c -> p (o c)")
                pe.wait_ge(band_made, 1)
                pe.matmul(bank[T2][:, 0:S], s_s[:, w.par, 0, 3 * P:4 * P], weights, start=True, stop=False)
                pe.matmul(bank[T2][:, P:S], s_s[:, w.par, 1, 3 * P:4 * P], weights1, start=False, stop=True).then_inc(r_pooled, 1)

            def r_scores(b, par, use):
                pe.wait_ge(bank_read[T1], USE0[T1]["rel"] + 2 * b + 1)
                pe.wait_ge(btile_made, b + 1)
                for hh in range(2):
                    free(X1 + hh, "rel", use if hh else 2 * b)
                    x, head = bank[X1 + hh], slice(AD * hh, AD * (hh + 1))
                    diagonal, off = btile[:, par, hh, 0, :], btile[:, par, hh, 1, :]
                    pe.matmul(x[:, 0:P], rqt_s[head, 0:P], rkt_s[head, 0:P], start=True, stop=False)
                    pe.matmul(x[:, 0:P], diagonal, anti[:], start=False, stop=True)
                    pe.matmul(x[:, P:P + S], rqt_s[head, P:S], rkt_s[head, :], start=True, stop=False)
                    pe.matmul(x[:, P:2 * P], off, anti[:], start=False, stop=False)
                    pe.matmul(x[:, 2 * P:3 * P], diagonal, anti[:], start=False, stop=True).then_inc(r_scored, 1)

            def r_weights_turn(b):
                pe.wait_ge(r_probs, b + 1)
                for hh in range(2):
                    free(T1 + hh, "rel", 2 * b + 1)
                    for n in range(3):
                        done = pe.transpose(bank[T1 + hh][:, n * P:(n + 1) * P], rp_s[:, hh, n * P:(n + 1) * P], ident[:])
                    done.then_inc(r_pturned, 1)

            def r_output(b, par):
                pe.wait_ge(bank_read[T1], USE0[T1]["rel"] + 2 * b + 2)
                pe.wait_ge(bank_read[T2], USE0[T2]["rel"] + 2 * b + 2)
                free(X1, "rel", 2 * b + 1)
                for hh in range(2):
                    o = bank[X1][AD * hh:AD * (hh + 1), :]
                    v = slice(2 * P + AD * hh, 2 * P + AD * (hh + 1))
                    pe.matmul(o[:, 0:S], s_s[:, par, 0, v], rpt_s[:, hh, 0:S], start=True, stop=False)
                    done = pe.matmul(o[:, P:S], s_s[:, par, 1, v], rpt_s[:, hh, S:S + P], start=False, stop=True)
                done.then_inc(r_out, 1)

            def pool_output(g):
                pe.wait_ge(pw_landed, g * 16 + 16)
                pe.wait_ge(bank_read[T2], USE0[T2]["rel"] + 4 * g + 3)
                free(X2, "rel", 3 * g + 2)
                for e in range(2):
                    for c in range(2):
                        done = pe.matmul(bank[X2][:, e * S:(e + 1) * S], pw[:, c, e * P:(e + 1) * P], dt_s[:, c, :],
                                         start=(c == 0), stop=(c == 1))
                done.then_inc(y_pool, 1)

            def rel_pieces(b, w, g, use, last=None, pooled=None):
                after = {1: [lambda: r_turn(b, w, g)], 3: [lambda: r_scores(b, w.par, use)], 6: [lambda: r_weights_turn(b)]}
                if last is not None:
                    after[0] = [lambda: r_output(last, 1 - w.par)]
                    if pooled is not None:
                        after[0].append(lambda: pool_output(pooled))
                return after

            w0, w1 = pair_windows("rel", 0)
            multiply(w0, zt_hi, zt_lo, before={6: [split_ready("gate", NB - 1)]}, after=gate_residual(NB - 1))
            multiply(w1, zt_hi, zt_lo, after=rel_pieces(0, w0, 0, 0))
            with pe.Fori(1, AH // 4) as i:
                _, before = pair_windows("rel", i - 1)
                w0, w1 = pair_windows("rel", i)
                multiply(w0, zt_hi, zt_lo, after=rel_pieces(2 * i - 1, before, i - 1, 3 * i - 2, 2 * i - 2))
                multiply(w1, zt_hi, zt_lo, after=rel_pieces(2 * i, w0, i, 3 * i, 2 * i - 1, i - 1))

            def mix_turn(n):
                return {1: [lambda: turn(lambda t, c: merged[:, t, c:c + P], "mix", n, merged_made, T * n + T)]}

            def mix_body(n, pieces, pieces_b={}, ready={}):
                ga, gb, ba, bb = mix_windows(n)
                multiply(ga, zt_hi, zt_lo, after=pieces)
                multiply(gb, zt_hi, zt_lo, after=pieces_b)
                multiply(ba, xt_hi, xt_lo, before=ready)
                multiply(bb, xt_hi, xt_lo, k0=AW // P)

            last = AH // 2 - 1
            _, before = pair_windows("rel", AH // 4 - 1)

            def mixers_split():
                pe.wait_ge(bank_read[X1], USE0[X1]["rel"] + 2 * last + 2)
                pe.wait_ge(bank_read[X2], USE0[X2]["rel"] + 3 * G)

            mix_body(0, rel_pieces(last, before, G - 1, 3 * G - 2, last - 1),
                     {0: [lambda: r_output(last, 1), lambda: pool_output(G - 1)]}, {0: [mixers_split]})
            with pe.Fori(1, NB) as n:
                mix_body(n, mix_turn(n - 1))
            ws = [w for i in range(NB // 2) for w in pair_windows("out2", i)]
            multiply(ws[0], mt_hi, mt_lo, before={6: [split_ready("mix", NB - 1)]}, after=mix_turn(NB - 1))
            for n in range(1, NB):
                multiply(ws[n], mt_hi, mt_lo, after=residual("out2", n - 1, ws[n - 1]))
            hidden_then_down("up2", "down2", "out2", ws[-1])

        @block.gpsimd
        def _(pool):
            def select(view, compare, fill, base, pattern, mult, made):
                pool.affine_select(out=view, in_=view, compare_op=compare, fill=fill, base=base, pattern=pattern,
                                   channel_multiplier=mult).then_inc(made, 1)

            pool.memset(ident[:], 0.0)
            pool.memset(anti[:], 0.0)
            pool.memset(ones[:], 1.0)
            pool.memset(half[:], -0.5)
            pool.memset(negs[:], NEG)
            pool.memset(mask_m[:], 0.0)
            pool.memset(mask_f[:], 0.0).then_inc(const_cleared, 1)
            pool.wait_ge(const_cleared, 1)
            select(ident[:], ALU.not_equal, 1.0, 0, [[-1, P]], 1, const_made)
            select(anti[:], ALU.not_equal, 1.0, 1 - P, [[1, P]], 1, const_made)
            for c in (0, S):
                select(mask_m[:, c:c + P], ALU.is_ge, NEG, 0, [[1, P]], -1, const_made)
            for c in (0, S):
                select(mask_f[:, c:c + P], ALU.is_ge, NEG, 0, [[-1, P]], 1, const_made)

            def norm(n):
                pool.wait_ge(meansq_done, n + 1)
                pool.tensor_scalar(meansq[:, n, :], meansq[:, n, :], 1.0 / D, EPS, ALU.mult, ALU.add).then_inc(meansq_eps, 1)
                pool.wait_ge(meansq_eps, n + 1)
                pool.tensor_tensor(rstd[:, n, :], meansq[:, n, :], half[:, 0:T], ALU.pow).then_inc(rstd_done, 1)

            norm(NORM["init"])

            pool.dma_start(bias_ext[:, 0:RB], A["rel_bias_2"][0]).then_inc(ext_landed, 16)
            pool.wait_ge(ext_landed, 16)
            pool.tensor_copy(bias_ext[:, RB:EXT], bias_ext[:, RB - 1:RB].to_broadcast([AH, EXT - RB])).then_inc(ext_made, 1)
            pool.wait_ge(ext_made, 1)
            pool.dma_start(bias_scratch, bias_ext[:]).then_inc(ext_stored, 16)
            pool.wait_ge(ext_stored, 16)

            pool.wait_ge(row_step, 5)
            for n, dst, row in ((MH, diag_m, 2), (FH, diag_f, 5)):
                src = crow[0:n, row:row + 1, :].to_broadcast([n, n, S])
                pool.affine_select(out=dst[:], in_=src, compare_op=ALU.is_equal, fill=0.0, base=0,
                                   pattern=[[1, n], [0, S]], channel_multiplier=-1).then_inc(diag_made, 1)

            def m_norm(h):
                pool.wait_ge(m_eps, h + 1)
                pool.tensor_tensor(M_RS, M_MS, half[:, 0:T], ALU.pow).then_inc(m_rs, 1)

            with pool.Fori(0, MH) as h:
                m_norm(h)

            def f_head(b, w):
                pool.wait_ge(acc_read[w.par], 2 * w.block + 2)
                qk = f_s[:, w.par, :, 0:2 * FD]
                pool.tensor_tensor(fsq_s[:], qk, qk, ALU.mult).then_inc(f_sq, 1)
                pool.wait_ge(f_eps, b + 1)
                pool.tensor_tensor(F_RS, F_SS, half[:], ALU.pow).then_inc(f_rs, 1)
                pool.wait_ge(f_rs, b + 1)
                for t in range(T):
                    done = pool.tensor_tensor(
                        fqk_s[:, t, :].rearrange("p (j d) -> p j d", d=FD), qk[:, t, :].rearrange("p (j d) -> p j d", d=FD),
                        F_RS[:, 2 * t:2 * t + 2].rearrange("p (j o) -> p j o", o=1).to_broadcast([P, 2, FD]), ALU.mult)
                done.then_inc(f_norm, 1)

            with pool.Fori(0, FH // 2) as i:
                for par, w in enumerate(fox_w(i)):
                    f_head(2 * i + par, w)
            norm(NORM["out"])
            pool.wait_ge(hid_lo, FF // W)
            pool.dma_start(p_s[:], A["p"][0, 0].rearrange("(t p) c -> p t c", p=P)).then_inc(p_landed, 16)
            norm(NORM["down"])

            pool.wait_ge(stage_used, proj_windows()[-1].end())
            for g, window in enumerate(POOL_WINDOWS):
                pool.memset(band[:, g, window - 1:S + P], 1.0 / window)
                for t in range(window - 1):
                    done = pool.memset(band[:, g, t:t + 1], 1.0 / (t + 1))
            done.then_inc(band_set, 1)
            pool.wait_ge(band_set, 1)
            for g, window in enumerate(POOL_WINDOWS):
                for cols_, n in ((slice(0, S), S), (slice(S, S + P), P)):
                    select(band[:, g, cols_], ALU.is_ge, 0.0, 0, [[1, n]], -1, band_set)
            pool.wait_ge(band_set, 1 + 2 * G)
            for g, window in enumerate(POOL_WINDOWS):
                for cols_, n in ((slice(0, S), S), (slice(S, S + P), P)):
                    select(band[:, g, cols_], ALU.is_ge, 0.0, window - 1, [[-1, n]], 1, band_set)
            pool.wait_ge(band_set, 1 + 4 * G)
            for g in range(G):
                for c in (0, S):
                    done = pool.tensor_tensor(band[:, g, c:c + P], band[:, g, c:c + P], ident[:], ALU.subtract)
            done.then_inc(band_made, 1)

            ext = bias_scratch.tensor
            diagonal = bass.AP(ext, 1, [[1, P], [EXT, AH], [1, P]])
            off = bass.AP(ext, 1 + P, [[1, P], [EXT, AH], [1, P]])

            def btiles(b, par):
                for kind, src in ((0, diagonal), (1, off)):
                    pool.dma_start(btile[:, par, :, kind, :], src[:, ds(2 * b, 2), :]).then_inc(btile_landed, 16)
                pool.wait_ge(btile_landed, 32 * b + 32)
                pool.tensor_tensor(btile[0:AD, par, :, 0, 0:AD], negs[0:AD].rearrange("p (h t) -> p h t", h=2),
                                   ones[0:AD, 0:P].rearrange("p (h t) -> p h t", h=2), ALU.mult).then_inc(btile_made, 1)

            def pool_weights(g):
                pool.dma_start(pw[:], A["pool_w_2"][0, ds(g, 1)].rearrange("o (k p) e -> p (o k) e", p=P)).then_inc(pw_landed, 16)

            btiles(0, 0)
            btiles(1, 1)
            pool_weights(0)
            norm(NORM["gate"])
            with pool.Fori(1, G) as g:
                for par in range(2):
                    pool.wait_ge(r_scored, 4 * g + 2 * par - 2)
                    btiles(2 * g + par, par)
                pool.wait_ge(y_pool, g)
                pool_weights(g)
            norm(NORM["out2"])
            norm(NORM["down2"])


_INS = ["x", "p", "mix_norm_g", "w_in", "mlstm_gate_bias", "mlstm_out_g", "fox_q_g", "fox_k_g", "fox_f_bias", "w_out",
        "ffn_norm_g", "w_up", "conv_w", "conv_b", "w_down", "ple_norm_g", "w_ple_gate", "w_ple_proj", "norm_mix_2",
        "w_in_2", "rel_bias_2", "pool_w_2", "pool_scale_2", "w_branch_a_2", "w_branch_b_2", "w_out_2", "norm_ffn_2",
        "w_gate_up_2", "w_down_2", "norm_final_2"]


def kernel(**inputs):
    import numpy as _np
    import concourse.bacc as _bacc
    from concourse import mybir as _mybir
    from concourse.bass_utils import run_bass_kernel_spmd as _run

    nc = _bacc.Bacc("TRN2", target_bir_lowering=False, num_devices=1)
    arrays, args = {}, {}
    for name in _INS:
        a = _np.ascontiguousarray(inputs[name])
        arrays[f"in_{name}_dram"] = a
        args[name] = nc.dram_tensor(f"in_{name}_dram", a.shape, _mybir.dt.from_np(a.dtype), kind="ExternalInput").ap()
    x = inputs["x"]
    out = nc.dram_tensor("out_0_dram", x.shape, _mybir.dt.from_np(_np.dtype("float32")), kind="ExternalOutput").ap()
    heads = inputs["rel_bias_2"].shape[1]
    scratch = nc.dram_tensor("bias_scratch", (heads, 3 * P), F32).ap()
    sandwich_kernel(nc, args, out, scratch)
    r = _run(nc, [arrays], core_ids=[0])
    return r.results[0]["out_0_dram"]
```
